# Optimizing a Trainium2 kernel written in Bass

```python
import math
import jax, jax.numpy as jnp
from jax import lax
import numpy as np

D_MODEL = 1024
BATCH = 1
SEQ = 512
DEPTH = 2

HEAD_DIM = 64
MLA_HEADS = 8
MLA_NOPE = 64
MLA_ROPE = 32
MLA_V = 64
MLA_Q_LORA = 384
MLA_KV_LORA = 256
ROPE_THETA = 10000.0
SWA_HEADS = 8
SWA_KV_HEADS = 2
SWA_WINDOW = 128
REL_BUCKETS = 32
REL_MAX_DIST = 128
FOX_HEADS = 16
D_FF = 4 * D_MODEL
D_PLE = 256
BLOCK_Q = 128
DN_ALPHA = (2 * DEPTH) ** 0.25
DN_BETA = (8 * DEPTH) ** -0.25
NORM_EPS = 1e-5
NEG_INF = -1e30
N_EVEN = (DEPTH + 1) // 2
N_ODD = DEPTH // 2
EVEN_SPLIT = (MLA_Q_LORA, MLA_KV_LORA, MLA_ROPE, SWA_HEADS * HEAD_DIM,
              SWA_KV_HEADS * HEAD_DIM, SWA_KV_HEADS * HEAD_DIM)
EVEN_IN = MLA_Q_LORA + MLA_KV_LORA + MLA_ROPE + (SWA_HEADS + 2 * SWA_KV_HEADS) * HEAD_DIM
EVEN_MIX = MLA_HEADS * MLA_V + SWA_HEADS * HEAD_DIM
ODD_SPLIT = (FOX_HEADS * HEAD_DIM, FOX_HEADS * HEAD_DIM, FOX_HEADS * HEAD_DIM, FOX_HEADS)
ODD_IN = 3 * FOX_HEADS * HEAD_DIM + FOX_HEADS
ODD_MIX = FOX_HEADS * HEAD_DIM


def _split(h, sizes):
    out, o = [], 0
    for n in sizes:
        out.append(h[..., o:o + n])
        o += n
    return out

def _layer_norm(x, g, b):
    xf = x.astype(jnp.float32)
    mu = jnp.mean(xf, -1, keepdims=True)
    var = jnp.mean(jnp.square(xf - mu), -1, keepdims=True)
    y = (xf - mu) * lax.rsqrt(var + NORM_EPS)
    return (y * g.astype(jnp.float32) + b.astype(jnp.float32)).astype(x.dtype)

def _rms_norm(x, g):
    xf = x.astype(jnp.float32)
    y = xf * lax.rsqrt(jnp.mean(jnp.square(xf), -1, keepdims=True) + NORM_EPS)
    return (y * g.astype(jnp.float32)).astype(x.dtype)

def _rope_tables(seq_len, dim):
    inv = 1.0 / (ROPE_THETA ** (jnp.arange(0, dim, 2, dtype=jnp.float32) / dim))
    ang = jnp.arange(seq_len, dtype=jnp.float32)[:, None] * inv[None, :]
    return jnp.cos(ang), jnp.sin(ang)

def _apply_rope(x, cos, sin):
    x1, x2 = jnp.split(x.astype(jnp.float32), 2, axis=-1)
    c = cos[:, None, :]
    s = sin[:, None, :]
    return jnp.concatenate([x1 * c - x2 * s, x2 * c + x1 * s], -1).astype(x.dtype)

def _t5_bucket(dist):
    exact = REL_BUCKETS // 2
    d = jnp.maximum(dist, 1).astype(jnp.float32)
    large = exact + (jnp.log(d / exact) / math.log(REL_MAX_DIST / exact)
                     * (REL_BUCKETS - exact)).astype(jnp.int32)
    large = jnp.minimum(large, REL_BUCKETS - 1)
    return jnp.where(dist < exact, dist, large)

def _mla_attend(q_nope, q_rope, k_nope, k_rope, v):
    B, S, H, _ = q_nope.shape
    nb = S // BLOCK_Q
    scale = (MLA_NOPE + MLA_ROPE) ** -0.5
    qn = q_nope.reshape(B, nb, BLOCK_Q, H, MLA_NOPE).transpose(1, 0, 2, 3, 4)
    qr = q_rope.reshape(B, nb, BLOCK_Q, H, MLA_ROPE).transpose(1, 0, 2, 3, 4)
    kpos = jnp.arange(S)

    def block(args):
        i, qn_b, qr_b = args
        s = (jnp.einsum('bqhd,bkhd->bhqk', qn_b, k_nope, preferred_element_type=jnp.float32)
             + jnp.einsum('bqhd,bkd->bhqk', qr_b, k_rope, preferred_element_type=jnp.float32)) * scale
        qpos = i * BLOCK_Q + jnp.arange(BLOCK_Q)
        s = jnp.where(kpos[None, :] <= qpos[:, None], s, NEG_INF)
        w = jax.nn.softmax(s, axis=-1).astype(v.dtype)
        return jnp.einsum('bhqk,bkhd->bqhd', w, v)

    out = lax.map(block, (jnp.arange(nb), qn, qr))
    return out.transpose(1, 0, 2, 3, 4).reshape(B, S, H * MLA_V)

def _swa_attend(q, k, v, sinks, rel_bias):
    B, S, H, d = q.shape
    KVH = k.shape[2]
    G = H // KVH
    nb = S // BLOCK_Q
    qb = q.reshape(B, nb, BLOCK_Q, KVH, G, d)

    def band(t):
        tb = t.reshape(B, nb, BLOCK_Q, KVH, d)
        prev = jnp.pad(tb, ((0, 0), (1, 0), (0, 0), (0, 0), (0, 0)))[:, :-1]
        return jnp.concatenate([prev, tb], axis=2)

    kb, vb = band(k), band(v)
    s = jnp.einsum('bnqkgd,bnskd->bnkgqs', qb, kb, preferred_element_type=jnp.float32) * (d ** -0.5)
    a = jnp.arange(BLOCK_Q)[:, None]
    col = jnp.arange(2 * BLOCK_Q)[None, :]
    dist = a + BLOCK_Q - col
    in_win = (dist >= 0) & (dist < SWA_WINDOW)
    pad = (jnp.arange(nb)[:, None, None] == 0) & (col < BLOCK_Q)[None]
    valid = in_win[None] & ~pad
    bias = rel_bias[_t5_bucket(jnp.maximum(dist, 0))].astype(jnp.float32)
    bias = bias.transpose(2, 0, 1).reshape(KVH, G, BLOCK_Q, 2 * BLOCK_Q)
    s = jnp.where(valid[None, :, None, None], s + bias, NEG_INF)
    sink = jnp.broadcast_to(sinks.astype(jnp.float32).reshape(1, 1, KVH, G, 1, 1), s.shape[:-1] + (1,))
    w = jax.nn.softmax(jnp.concatenate([s, sink], axis=-1), axis=-1)[..., :-1].astype(v.dtype)
    out = jnp.einsum('bnkgqs,bnskd->bnqkgd', w, vb)
    return out.reshape(B, S, H * d)

def _fox_attend(q, k, v, log_f):
    B, S, H, d = q.shape
    nb = S // BLOCK_Q
    c = jnp.cumsum(log_f, axis=1)
    cq = c.reshape(B, nb, BLOCK_Q, H).transpose(1, 0, 3, 2)
    ck = c.transpose(0, 2, 1)
    qb = q.reshape(B, nb, BLOCK_Q, H, d).transpose(1, 0, 2, 3, 4)
    kpos = jnp.arange(S)

    def block(args):
        i, q_b, cq_b = args
        s = jnp.einsum('bqhd,bkhd->bhqk', q_b, k, preferred_element_type=jnp.float32) * (d ** -0.5)
        s = s + cq_b[..., :, None] - ck[:, :, None, :]
        qpos = i * BLOCK_Q + jnp.arange(BLOCK_Q)
        s = jnp.where(kpos[None, :] <= qpos[:, None], s, NEG_INF)
        w = jax.nn.softmax(s, axis=-1).astype(v.dtype)
        return jnp.einsum('bhqk,bkhd->bqhd', w, v)

    out = lax.map(block, (jnp.arange(nb), qb, cq))
    return out.transpose(1, 0, 2, 3, 4).reshape(B, S, H * d)

def _even_mixer(x, w_in, q_norm, w_uq, kv_norm, w_ukv, sinks, w_out, rel_bias, cos, sin):
    B, S, _ = x.shape
    h = x @ w_in
    c_q, c_kv, k_rope, q_s, k_s, v_s = _split(h, EVEN_SPLIT)
    q = (_rms_norm(c_q, q_norm) @ w_uq).reshape(B, S, MLA_HEADS, MLA_NOPE + MLA_ROPE)
    q_nope = q[..., :MLA_NOPE]
    q_rope = _apply_rope(q[..., MLA_NOPE:], cos, sin)
    kv = (_rms_norm(c_kv, kv_norm) @ w_ukv).reshape(B, S, MLA_HEADS, MLA_NOPE + MLA_V)
    k_nope, v = kv[..., :MLA_NOPE], kv[..., MLA_NOPE:]
    k_rope = _apply_rope(k_rope[:, :, None, :], cos, sin)[:, :, 0]
    o_mla = _mla_attend(q_nope, q_rope, k_nope, k_rope, v)
    o_swa = _swa_attend(q_s.reshape(B, S, SWA_HEADS, HEAD_DIM),
                        k_s.reshape(B, S, SWA_KV_HEADS, HEAD_DIM),
                        v_s.reshape(B, S, SWA_KV_HEADS, HEAD_DIM), sinks, rel_bias)
    return jnp.concatenate([o_mla, o_swa], axis=-1) @ w_out

def _odd_mixer(x, w_in, b_f, w_out):
    B, S, _ = x.shape
    q, k, v, f = _split(x @ w_in, ODD_SPLIT)
    log_f = jax.nn.log_sigmoid((f + b_f).astype(jnp.float32))
    o = _fox_attend(q.reshape(B, S, FOX_HEADS, HEAD_DIM), k.reshape(B, S, FOX_HEADS, HEAD_DIM),
                    v.reshape(B, S, FOX_HEADS, HEAD_DIM), log_f)
    return o @ w_out

def _sq_relu_mlp(x, w_up, w_down):
    return jnp.square(jax.nn.relu(x @ w_up)) @ w_down

def first_inputs(seed: int = 0) -> dict:
    key = jax.random.key(seed)
    ks = jax.random.split(key, 24)
    nrm = jax.random.normal
    f32 = jnp.float32
    return {
        "x": nrm(ks[0], (BATCH, SEQ, D_MODEL), f32),
        "p": nrm(ks[1], (DEPTH, BATCH, SEQ, D_PLE), f32),
        "rel_bias": 0.5 * nrm(ks[2], (REL_BUCKETS, SWA_HEADS), f32),
        "ev_w_in": nrm(ks[3], (N_EVEN, D_MODEL, EVEN_IN), f32) * D_MODEL ** -0.5,
        "ev_q_norm": 1.0 + 0.02 * nrm(ks[4], (N_EVEN, MLA_Q_LORA), f32),
        "ev_w_uq": nrm(ks[5], (N_EVEN, MLA_Q_LORA, MLA_HEADS * (MLA_NOPE + MLA_ROPE)), f32) * MLA_Q_LORA ** -0.5,
        "ev_kv_norm": 1.0 + 0.02 * nrm(ks[6], (N_EVEN, MLA_KV_LORA), f32),
        "ev_w_ukv": nrm(ks[7], (N_EVEN, MLA_KV_LORA, MLA_HEADS * (MLA_NOPE + MLA_V)), f32) * MLA_KV_LORA ** -0.5,
        "ev_sinks": 0.5 * nrm(ks[8], (N_EVEN, SWA_HEADS), f32),
        "ev_w_out": nrm(ks[9], (N_EVEN, EVEN_MIX, D_MODEL), f32) * (EVEN_MIX ** -0.5 * DN_BETA),
        "od_w_in": nrm(ks[10], (N_ODD, D_MODEL, ODD_IN), f32) * D_MODEL ** -0.5,
        "od_b_f": jax.random.uniform(ks[11], (N_ODD, FOX_HEADS), f32, 1.0, 4.0),
        "od_w_out": nrm(ks[12], (N_ODD, ODD_MIX, D_MODEL), f32) * (ODD_MIX ** -0.5 * DN_BETA),
        "ln1_g": 1.0 + 0.02 * nrm(ks[13], (DEPTH, D_MODEL), f32),
        "ln1_b": 0.02 * nrm(ks[14], (DEPTH, D_MODEL), f32),
        "w_up": nrm(ks[15], (DEPTH, D_MODEL, D_FF), f32) * D_MODEL ** -0.5,
        "w_down": nrm(ks[16], (DEPTH, D_FF, D_MODEL), f32) * (D_FF ** -0.5 * DN_BETA),
        "ln2_g": 1.0 + 0.02 * nrm(ks[17], (DEPTH, D_MODEL), f32),
        "ln2_b": 0.02 * nrm(ks[18], (DEPTH, D_MODEL), f32),
        "ple_w_proj": nrm(ks[19], (DEPTH, D_PLE, D_MODEL), f32) * D_PLE ** -0.5,
        "ple_w_gate": nrm(ks[20], (DEPTH, D_MODEL, D_MODEL), f32) * D_MODEL ** -0.5,
        "ple_b_gate": 0.02 * nrm(ks[21], (DEPTH, D_MODEL), f32),
    }

def first_block(x, p, rel_bias, ev_w_in, ev_q_norm, ev_w_uq, ev_kv_norm, ev_w_ukv, ev_sinks, ev_w_out,
              od_w_in, od_b_f, od_w_out, ln1_g, ln1_b, w_up, w_down, ln2_g, ln2_b,
              ple_w_proj, ple_w_gate, ple_b_gate):
    S = x.shape[1]
    cos, sin = _rope_tables(S, MLA_ROPE)
    for i in range(DEPTH):
        j = i // 2
        if i % 2 == 0:
            m = _even_mixer(x, ev_w_in[j], ev_q_norm[j], ev_w_uq[j], ev_kv_norm[j], ev_w_ukv[j],
                            ev_sinks[j], ev_w_out[j], rel_bias, cos, sin)
        else:
            m = _odd_mixer(x, od_w_in[j], od_b_f[j], od_w_out[j])
        x = _layer_norm(DN_ALPHA * x + m, ln1_g[i], ln1_b[i])
        x = _layer_norm(DN_ALPHA * x + _sq_relu_mlp(x, w_up[i], w_down[i]), ln2_g[i], ln2_b[i])
        gate = jax.nn.sigmoid(x @ ple_w_gate[i] + ple_b_gate[i])
        x = x + gate * (p[i] @ ple_w_proj[i])
    return x


DEPTH_2 = 1

CHUNK = 64
N_BRANCH = 4
BRANCH_W = D_MODEL // N_BRANCH
RMS_EPS = 1e-6
NEG_BIG = -1e30
LOG_FLOOR = 1e-30
HG_HEADS = 4
HG_DK = 128
HG_DV = BRANCH_W // HG_HEADS
POOL_WINDOWS = (2, 4, 8, 16)
POOL_GROUP = BRANCH_W // len(POOL_WINDOWS)
SA_HEADS = 4
SA_DH = BRANCH_W // SA_HEADS
IDX_HEADS = 8
IDX_DH = 64
TOPK_MAX = 256
Q_BLOCK = 128
N_MEM = 256
MEM_HEADS = 4
MEM_DH = BRANCH_W // MEM_HEADS
D_FF_2 = -(-8 * D_MODEL // (3 * 256)) * 256
SPLIT_SIZES = (HG_HEADS * HG_DK, HG_HEADS * HG_DK, BRANCH_W, BRANCH_W,
               BRANCH_W,
               SA_HEADS * SA_DH, SA_DH, SA_DH,
               IDX_HEADS * IDX_DH, IDX_DH, IDX_HEADS,
               MEM_HEADS * MEM_DH)
N_IN = sum(SPLIT_SIZES)


F32 = jnp.float32

def rms_norm(x, gain, eps=RMS_EPS):
    xf = x.astype(F32)
    y = xf * lax.rsqrt(jnp.mean(xf * xf, axis=-1, keepdims=True) + eps)
    return (y * gain.astype(F32)).astype(x.dtype)

def hgrn2_mixer(q, f_logit, i, g, lb, o_gain):
    B, T, _ = q.shape
    n = T // CHUNK
    lbf = lb.astype(F32)
    sg = jax.nn.sigmoid(f_logit.astype(F32))
    f = lbf + (1.0 - lbf) * sg
    log_f = jnp.log(jnp.maximum(f, LOG_FLOOR))
    k = (1.0 - lbf) * (1.0 - sg)
    qf = jax.nn.silu(q.astype(F32))

    def to_chunks(a, d):
        return a.reshape(B, n, CHUNK, HG_HEADS, d).transpose(1, 0, 2, 3, 4)

    xs = (to_chunks(qf, HG_DK), to_chunks(k, HG_DK), to_chunks(log_f, HG_DK),
          to_chunks(i.astype(F32), HG_DV))
    causal = jnp.tril(jnp.ones((CHUNK, CHUNK), dtype=bool))[None, :, :, None, None]

    def step(S, inp):
        qc, kc, lfc, vc = inp
        b = jnp.cumsum(lfc, axis=1)
        o_inter = jnp.einsum('bthk,bhkv->bthv', qc * jnp.exp(b), S)
        diff = jnp.where(causal, b[:, :, None] - b[:, None, :], 0.0)
        decay = jnp.where(causal, jnp.exp(diff), 0.0)
        att = jnp.einsum('bthk,bshk,btshk->bhts', qc, kc, decay)
        o_intra = jnp.einsum('bhts,bshv->bthv', att, vc)
        b_last = b[:, -1]
        S = jnp.exp(b_last)[..., None] * S + jnp.einsum(
            'bshk,bshv->bhkv', kc * jnp.exp(b_last[:, None] - b), vc)
        return S, o_inter + o_intra

    S0 = jnp.zeros((B, HG_HEADS, HG_DK, HG_DV), F32)
    _, o = lax.scan(step, S0, xs)
    o = o.transpose(1, 0, 2, 3, 4).reshape(B, T, HG_HEADS, HG_DV)
    o = o * lax.rsqrt(jnp.mean(o * o, axis=-1, keepdims=True) + RMS_EPS)
    o = o.reshape(B, T, BRANCH_W) * o_gain.astype(F32) * jax.nn.silu(g.astype(F32))
    return o.astype(q.dtype)

def pool_mixer(z, pool_w, pool_scale):
    B, T, _ = z.shape
    zf = z.astype(F32).reshape(B, T, len(POOL_WINDOWS), POOL_GROUP)
    csum = jnp.cumsum(zf, axis=1)
    pos = jnp.arange(T)
    means = []
    for gi, w in enumerate(POOL_WINDOWS):
        c = csum[:, :, gi]
        lagged = jnp.pad(c, ((0, 0), (w, 0), (0, 0)))[:, :T]
        cnt = jnp.minimum(pos + 1, w).astype(F32)
        means.append((c - lagged) / cnt[None, :, None])
    pooled = jnp.stack(means, axis=2) - zf
    y = jnp.einsum('btgc,gcd->btgd', pooled, pool_w.astype(F32)).reshape(B, T, BRANCH_W)
    return (y * pool_scale.astype(F32)).astype(z.dtype)

def dsa_mixer(q, k, v, iq, ik, iw):
    B, T, _ = q.shape
    n_sel = min(TOPK_MAX, T // 4)
    nb = T // Q_BLOCK

    def blocks(a, tail):
        return jnp.moveaxis(a.reshape((B, nb, Q_BLOCK) + tail), 1, 0)

    qb_all = blocks(q, (SA_HEADS, SA_DH))
    iqb_all = blocks(iq, (IDX_HEADS, IDX_DH))
    iwb_all = blocks(iw, (IDX_HEADS,))
    key_pos = jnp.arange(T)
    gather = jax.vmap(lambda arr, idx: arr[idx])

    def block(args):
        bi, qb, iqb, iwb = args
        qpos = bi * Q_BLOCK + jnp.arange(Q_BLOCK)
        limit = (qpos // CHUNK + 1) * CHUNK
        admissible = key_pos[None, :] < limit[:, None]
        logits = jnp.einsum('bqhd,bsd->bqsh', iqb, ik).astype(F32) * (IDX_DH ** -0.5)
        score = jnp.einsum('bqsh,bqh->bqs', jax.nn.relu(logits),
                           iwb.astype(F32) * (IDX_HEADS ** -0.5))
        score = jnp.where(admissible[None], score, NEG_BIG)
        top_val, top_idx = lax.top_k(score, n_sel)
        valid = top_val > 0.5 * NEG_BIG
        k_sel = gather(k, top_idx)
        v_sel = gather(v, top_idx)
        s = jnp.einsum('bqhd,bqkd->bhqk', qb, k_sel).astype(F32) * (SA_DH ** -0.5)
        s = jnp.where(valid[:, None], s, NEG_BIG)
        p = jax.nn.softmax(s, axis=-1)
        o = jnp.einsum('bhqk,bqkd->bqhd', p.astype(v.dtype), v_sel)
        return o.reshape(B, Q_BLOCK, SA_HEADS * SA_DH)

    out = lax.map(block, (jnp.arange(nb), qb_all, iqb_all, iwb_all))
    return jnp.moveaxis(out, 0, 1).reshape(B, T, SA_HEADS * SA_DH)

def mem_attention(qm, mk, mv):
    B, T, _ = qm.shape
    qh = qm.reshape(B, T, MEM_HEADS, MEM_DH)
    kh = mk.reshape(B, N_MEM, MEM_HEADS, MEM_DH)
    vh = mv.reshape(B, N_MEM, MEM_HEADS, MEM_DH)
    s = jnp.einsum('bthd,bnhd->bhtn', qh, kh).astype(F32) * (MEM_DH ** -0.5)
    p = jax.nn.softmax(s, axis=-1)
    o = jnp.einsum('bhtn,bnhd->bthd', p.astype(vh.dtype), vh)
    return o.reshape(B, T, MEM_HEADS * MEM_DH)

def second_inputs(seed: int = 0) -> dict:
    key = jax.random.key(seed)
    ks = jax.random.split(key, 18)
    L, D = DEPTH_2, D_MODEL
    nrm = lambda k, shape, fan: jax.random.normal(k, shape, F32) * (fan ** -0.5)
    gain = lambda k, shape: 1.0 + 0.1 * jax.random.normal(k, shape, F32)
    return {
        "x": jax.random.normal(ks[0], (BATCH, SEQ, D), F32),
        "mem": jax.random.normal(ks[1], (BATCH, N_MEM, D), F32),
        "lb_logits": jax.random.normal(ks[2], (L, HG_HEADS * HG_DK), F32),
        "w_in": nrm(ks[3], (L, D, N_IN), D),
        "w_gate": nrm(ks[4], (L, N_BRANCH, D, D), D),
        "w_branch": nrm(ks[5], (L, N_BRANCH, BRANCH_W, D), BRANCH_W),
        "w_out": nrm(ks[6], (L, D, D), D),
        "hgrn_norm": gain(ks[7], (L, BRANCH_W)),
        "pool_w": nrm(ks[8], (L, len(POOL_WINDOWS), POOL_GROUP, POOL_GROUP), POOL_GROUP),
        "pool_scale": gain(ks[9], (L, BRANCH_W)),
        "w_mem_kv": nrm(ks[10], (L, D, 2 * MEM_HEADS * MEM_DH), D),
        "norm_mem": gain(ks[11], (L, D)),
        "norm_mix_pre": gain(ks[12], (L, D)),
        "norm_mix_post": gain(ks[13], (L, D)),
        "norm_ffn_pre": gain(ks[14], (L, D)),
        "norm_ffn_post": gain(ks[15], (L, D)),
        "w_ffn_gate_up": nrm(ks[16], (L, D, 2 * D_FF_2), D),
        "w_ffn_down": nrm(ks[17], (L, D_FF_2, D), D_FF_2),
    }

def second_block(x, mem, lb_logits, w_in, w_gate, w_branch, w_out, hgrn_norm, pool_w,
              pool_scale, w_mem_kv, norm_mem, norm_mix_pre, norm_mix_post,
              norm_ffn_pre, norm_ffn_post, w_ffn_gate_up, w_ffn_down):
    split_pts = [int(p) for p in np.cumsum(SPLIT_SIZES)[:-1]]
    lb_soft = jax.nn.softmax(lb_logits.astype(F32), axis=0)
    lb_all = jnp.cumsum(lb_soft, axis=0) - lb_soft[0:1]
    h = x
    for l in range(DEPTH_2):
        u = rms_norm(h, norm_mix_pre[l])
        z = u @ w_in[l]
        (hq, hf, hi, hg, pz, sq, sk, sv, iq, ik, iw, mq) = jnp.split(z, split_pts, axis=-1)
        y_a = hgrn2_mixer(hq, hf, hi, hg, lb_all[l], hgrn_norm[l])
        y_b = pool_mixer(pz, pool_w[l], pool_scale[l])
        y_c = dsa_mixer(sq, sk, sv, iq, ik, iw)
        mkv = rms_norm(mem, norm_mem[l]) @ w_mem_kv[l]
        mk, mv = jnp.split(mkv, 2, axis=-1)
        y_m = mem_attention(mq, mk, mv)
        merged = None
        for bi, y in enumerate((y_a, y_b, y_c, y_m)):
            term = jax.nn.sigmoid(u @ w_gate[l, bi]) * (y @ w_branch[l, bi])
            merged = term if merged is None else merged + term
        h = h + rms_norm(merged @ w_out[l], norm_mix_post[l])
        u = rms_norm(h, norm_ffn_pre[l])
        gt, up = jnp.split(u @ w_ffn_gate_up[l], 2, axis=-1)
        h = h + rms_norm((jax.nn.silu(gt) * up) @ w_ffn_down[l], norm_ffn_post[l])
    return h


def setup_inputs(seed=0):
    out = dict(first_inputs(seed))
    for name, value in second_inputs(seed + 1).items():
        if name != "x":
            out[name + "_2"] = value
    return out


def reference(
    x, p, rel_bias, ev_w_in, ev_q_norm, ev_w_uq, ev_kv_norm, ev_w_ukv, ev_sinks, ev_w_out,
    od_w_in, od_b_f, od_w_out, ln1_g, ln1_b, w_up, w_down, ln2_g, ln2_b, ple_w_proj, ple_w_gate,
    ple_b_gate, mem_2, lb_logits_2, w_in_2, w_gate_2, w_branch_2, w_out_2, hgrn_norm_2,
    pool_w_2, pool_scale_2, w_mem_kv_2, norm_mem_2, norm_mix_pre_2, norm_mix_post_2,
    norm_ffn_pre_2, norm_ffn_post_2, w_ffn_gate_up_2, w_ffn_down_2,
):
    x = first_block(
        x, p, rel_bias, ev_w_in, ev_q_norm, ev_w_uq, ev_kv_norm, ev_w_ukv, ev_sinks, ev_w_out,
        od_w_in, od_b_f, od_w_out, ln1_g, ln1_b, w_up, w_down, ln2_g, ln2_b, ple_w_proj,
        ple_w_gate, ple_b_gate,
    )
    return second_block(
        x, mem_2, lb_logits_2, w_in_2, w_gate_2, w_branch_2, w_out_2, hgrn_norm_2, pool_w_2,
        pool_scale_2, w_mem_kv_2, norm_mem_2, norm_mix_pre_2, norm_mix_post_2, norm_ffn_pre_2,
        norm_ffn_post_2, w_ffn_gate_up_2, w_ffn_down_2,
    )


_drawn_inputs = setup_inputs


def setup_inputs(seed=0):
    import zlib

    import numpy as np

    out = dict(_drawn_inputs(seed))
    spreads = {}
    factors = {'ev_q_norm': 8.0,
     'ev_kv_norm': 8.0,
     'ev_sinks': 59.196,
     'ple_b_gate': 5.858,
     'norm_mem_2': 4.621,
     'rel_bias': 3.662,
     'hgrn_norm_2': 4.006,
     'pool_scale_2': 2.9}
    for name, (base, spread) in spreads.items():
        noise = np.random.default_rng([zlib.crc32(name.encode()), seed]).standard_normal(out[name].shape)
        drawn = base * np.exp(spread * noise) if base else spread * noise
        out[name] = __import__('jax').numpy.asarray(drawn.astype(out[name].dtype))
    for name, factor in factors.items():
        out[name] = (out[name] * factor).astype(out[name].dtype)
    return out
```

```python
import math
from contextlib import ExitStack

import numpy as np
import concourse.bass as bass
from concourse import mybir

F32, F32R, BF16, I32 = mybir.dt.float32, mybir.dt.float32r, mybir.dt.bfloat16, mybir.dt.int32
ALU, ACT, AX = mybir.AluOpType, mybir.ActivationFunctionType, mybir.AxisListType
P = 128
T = 512
D = 1024
DT = D // P
TT = T // P
DFF = 4096
DFF2 = 2816
NMEM = 256
NEG = -1e30
ALPHA = 4 ** 0.25
HID = (12, 10)
TOPN = 128

C_ID, C_CAUS, C_CHUNK, C_ANTI, C_SWAP, C_COS, C_SIN, C_OH = 0, 128, 256, 384, 512, 608, 1120, 1632
C_A = 2016
C_MASK, C_BONE, C_CNT = 0, 1024, 1152
C_B = 2176


def shape_tables():
    a = np.zeros((P, C_A), np.float32)
    i = np.arange(P)
    a[:, C_ID:C_ID + P] = np.eye(P)
    a[:, C_CAUS:C_CAUS + P] = np.where(i[None] <= i[:, None], 0.0, NEG)
    a[:, C_CHUNK:C_CHUNK + P] = np.where(i[None] < (i[:, None] // 64 + 1) * 64, 0.0, NEG)
    a[:, C_ANTI:C_ANTI + P] = np.eye(P)[::-1]
    for m in range(16):
        a[80 + m, C_SWAP + 64 + m] = -1.0
        a[64 + m, C_SWAP + 80 + m] = 1.0
    inv = (np.float32(1.0) / (np.float32(10000.0) ** (np.arange(0, 32, 2, dtype=np.float32) / np.float32(32)))).astype(np.float32)
    ang = (np.arange(T, dtype=np.float32)[:, None] * inv[None]).astype(np.float32)
    a[64:96, C_COS:C_COS + T] = np.concatenate([np.cos(ang), np.cos(ang)], 1).T
    a[64:96, C_SIN:C_SIN + T] = np.concatenate([np.sin(ang), np.sin(ang)], 1).T
    for j in range(383):
        d = 255 - j
        if 0 <= d < 128:
            large = 16 + int(np.float32(np.log(np.float32(max(d, 1)) / np.float32(16)) / math.log(8.0) * 16))
            a[d if d < 16 else min(large, 31), C_OH + j] = 1.0
        else:
            a[32, C_OH + j] = 1.0
    b = np.zeros((P, C_B), np.float32)
    for l in range(7):
        h = 1 << l
        blk, half = i // (2 * h), (i // h) % 2
        b[:, C_MASK + l * P:C_MASK + (l + 1) * P] = (blk[:, None] == blk[None]) & (half[:, None] == 0) & (half[None] == 1)
    b[:, C_MASK + 7 * P:C_MASK + 8 * P] = np.eye(P)
    b[:, C_BONE:C_BONE + P] = i[:, None] // 64 == i[None] // 64
    t = np.arange(T)
    for g, w in enumerate((2, 4, 8, 16)):
        b[(g % 2) * 64:(g % 2) * 64 + 64, C_CNT + (g // 2) * T:C_CNT + (g // 2 + 1) * T] = 1.0 / np.minimum(t + 1, w)
    return a, b


class Counts:

    def __init__(self, known):
        self.known, self.now, self.found = known, {}, {}

    def note(self, sem, key):
        self.now[sem] = self.now.get(sem, 0) + 1
        assert (sem, key) not in self.found, (sem, key)
        self.found[sem, key] = self.now[sem]

    def value(self, sem, key):
        return self.known[sem, key] if self.known is not None else 1


SEMS = """const_in x_in small_in relb_in band_out band_in aug_in aug2_in y_out p_in xt ident x_hi x_lo zeroed misc
 misc_free sq kr rs_ln rs_exp rsq norm n_hi n_lo qrope scores score_free biased rowmax probs probs_n ptrans
 ptev pv o_hi o_lo sinkexp bandv sum7 sum8 mean cen sqr var ln_t x_new h_relu h_sq h_hi h_lo fl fox_c chain_d
 chain_a chain_p out_t gate_t gate_s pt_hi mem_in tabb_in sq2 rn r_hi r_lo pooled pw_in y_hi y_lo ix ixr ixs
 topk hsp hg_x hg_prod hg_read hg_e hg_d hg_o hg_small hx""".split()


def program(nc, known, t):
    cnt = Counts(known)
    ctx = ExitStack()
    with ctx:
        sem = {n: ctx.enter_context(nc.semaphore(n)) for n in SEMS}
        loaded = [ctx.enter_context(nc.semaphore(f"loaded{s}")) for s in range(4)]
        hi_done = [ctx.enter_context(nc.semaphore(f"hi_done{s}")) for s in range(4)]
        lo_done = [ctx.enter_context(nc.semaphore(f"lo_done{s}")) for s in range(4)]
        used = [ctx.enter_context(nc.semaphore(f"used{s}")) for s in range(4)]
        evac = [ctx.enter_context(nc.semaphore(f"evac{b}")) for b in range(2)]
        PB = [ctx.enter_context(nc.psum_tensor(f"PB{i}", [P, T], F32)) for i in range(8)]

        base = nc.sbuf_base
        top = [(base + 63) // 64 * 64]

        def at(name, shape, dt, off):
            return nc.alloc_sbuf_tensor_at(name, shape, dt, offset=off)

        def sb(name, shape, dt):
            size = (int(np.prod(shape[1:])) * (2 if dt == BF16 else 4) + 31) // 32 * 32
            h = at(name, shape, dt, top[0])
            top[0] += size
            return h

        RAW = sb("RAW", [P, 4, 8, P], F32)
        WH = sb("WH", [P, 4, 8, P], F32R)
        WL = sb("WL", [P, 4, 8, P], F32R)
        X = sb("X", [P, DT, T], F32)
        xh_at = top[0]
        XH = sb("XH", [P, DT, T], F32R)
        XL = sb("XL", [P, DT, T], F32R)
        acc_at = top[0]
        ACC = sb("ACC", [P, DT, T], F32)
        ID = sb("ID", [P, P], F32)
        ID16 = sb("ID16", [P, P], BF16)
        CA16 = sb("CA16", [P, P], BF16)
        ONES = sb("ONES", [P, P], F32)
        VEC = sb("VEC", [P, 128], F32)
        HB = sb("HB", [P, 16], F32)
        STAT = sb("STAT", [P, 64], F32)
        VEC2 = sb("VEC2", [P, 64], F32)
        LBV = sb("LBV", [P, 8, 4], F32)
        EPS5 = sb("EPS5", [P, 1], F32)
        EPS6 = sb("EPS6", [P, 1], F32)
        arena = top[0]

        def region(name, shape, dt):
            return sb(name, shape, dt)

        PR = region("PR", [P, 2, T], F32)
        PT = region("PT", [P, 2, TT, T], F32)
        RS = region("RS", [P, T], F32)
        TMP = region("TMP", [P, T], F32)
        VT = region("VT", [P, T], F32)
        mixer = top[0]
        CST = region("CST", [P, C_A - 384], F32)
        latent_at = top[0]
        CQH = region("CQH", [P, 3, T], F32R)
        CQL = region("CQL", [P, 3, T], F32R)
        CKH = region("CKH", [P, 2, T], F32R)
        CKL = region("CKL", [P, 2, T], F32R)
        KR = at("KR", [96, T], F32, top[0] - 0)
        top[0] += 2048
        QS = region("QS", [P, 4, T], F32)
        K2 = region("K2", [P, 2, T], F32)
        VS = region("VS", [P, TT, P], F32)
        K96 = region("K96", [96, 8, T], F32)
        V4 = at("V4", [P, TT, T], F32, latent_at)
        Q96 = at("Q96", [96, 8, T], F32, acc_at)
        BIAS = region("BIAS", [P, 8, 256], F32)
        end_a = top[0]
        BAND = at("BAND", [P, 8, 256], F32, end_a - 8192 - 16384)
        top[0] = arena
        HR = region("HR", [P, 2, T], F32)
        HS = region("HS", [P, 2, T], F32)
        HH = region("HH", [P, 16, T], F32R)
        HL = region("HL", [P, 16, T], F32R)
        end_b = top[0]
        XIN = at("XIN", [P, TT, D], F32, acc_at)
        top[0] = mixer
        QA = region("QA", [66, 2, 2, T], F32)
        KA = region("KA", [66, 2, 2, T], F32)
        VP = region("VP", [P, 2, TT, P], F32)
        FZ = region("FZ", [16, 5, T], F32)
        OH = region("OH", [P, DT, T], F32R)
        OL = region("OL", [P, DT, T], F32R)
        end_c = top[0]
        top[0] = arena
        PIN = at("PIN", [P, TT, 256], F32, end_b)
        PTH = at("PTH", [P, 2, T], F32R, end_b + 4096)
        PTL = at("PTL", [P, 2, T], F32R, end_b + 8192)
        SM = at("SM", [P, 2, T], F32, arena + 88 * 1024)
        GT = at("GT", [P, 2, T], F32, arena + 12288)
        GP = at("GP", [P, 2, T], F32, arena + 16384)
        OUTT = at("OUTT", [P, 2, TT, T], F32, xh_at)
        assert max(end_a, end_b, end_c) <= nc.sbuf_usable_end, (end_a, end_b, end_c, nc.sbuf_usable_end)
        top[0] = mixer
        YH = region("YH", [P, 4, 2, T], F32R)
        YL = region("YL", [P, 4, 2, T], F32R)
        zone = top[0]
        MQ = region("MQ", [P, 2, T], F32)
        MK = region("MK", [P, 2, NMEM], F32)
        MV = region("MV", [P, 2, NMEM], F32)
        zone2 = top[0]
        SQ_ = region("SQ_", [P, 2, T], F32)
        SK2 = region("SK2", [P, T], F32)
        SV = region("SV", [P, TT, 64], F32)
        CHK = region("CHK", [P, P], F32)
        IWT = region("IWT", [P, TT, 8], F32)
        top[0] = zone2 + 8192
        IQ = region("IQ", [P, 4, T], F32)
        IK2 = region("IK2", [P, T], F32)
        SC = region("SC", [P, 3, T], F32)
        MSK = at("MSK", [P, TT, T], BF16, mixer + 16384)
        end_d = top[0]
        HV = at("HV", [P, TT, NMEM], F32, zone)
        HG = at("HG", [P, 2, T], F32, zone + 4096)
        top[0] = zone2
        QQ = region("QQ", [P, 4, T], F32)
        FC = region("FC", [P, 4, T], F32)
        KK = region("KK", [P, 4, T], F32)
        LMASK = at("LMASK", [P, 8, P], F32, mixer + 16384)
        BONE = region("BONE", [P, P], F32)
        OFF = region("OFF", [P, 3, 4, 8], F32)
        end_e = top[0]
        EE = at("EE", [P, 4, T], F32, acc_at)
        XX = at("XX", [P, 4, T], F32, acc_at + 8192)
        ATT = at("ATT", [P, 4, 10, P], F32, arena)
        MIN = at("MIN", [P, 2, D], F32, acc_at)
        MT = at("MT", [P, DT, NMEM], F32, acc_at + 8192)
        MH = at("MH", [P, DT, NMEM], F32R, mixer)
        ML = at("ML", [P, DT, NMEM], F32R, mixer + 8192)
        SQM = at("SQM", [P, DT, NMEM], F32, arena)
        SQX = at("SQX", [P, DT, T], F32, arena)
        PZ = at("PZ", [P, 2, 528], F32, arena)
        PA = at("PA", [P, 2, 528], F32, arena + 4224)
        PBf = at("PBf", [P, 2, 528], F32, arena + 8448)
        PO = at("PO", [P, 2, T], F32, arena + 12672)
        CNT = at("CNT", [P, 2, T], F32, zone2)
        PW = at("PW", [P, 2, 64], F32, arena + 16768)
        OO = at("OO", [P, 2, T], F32, acc_at)
        OS = at("OS", [P, 2, T], F32, acc_at + 4096)
        H2 = at("H2", [P, 12, T], F32R, arena + 12288 + 8192)
        L2 = at("L2", [P, 12, T], F32R, arena + 12288 + 8192 + 24576)
        GT2 = at("GT2", [P, 2, T], F32, arena)
        HS2 = at("HS2", [P, 4, T], F32, arena + 4096)
        assert max(end_d, end_e) <= nc.sbuf_usable_end, (end_d, end_e, nc.sbuf_usable_end)
        band_dram = nc.dram_tensor("band_scratch", (8, 384), F32).ap()

        VCOL, c = {}, 0
        vec_src = [("ev_q_norm", 0, 3), ("ev_kv_norm", 0, 2)]
        for l in range(2):
            vec_src += [("ln1_g", l, 8), ("ln1_b", l, 8), ("ln2_g", l, 8), ("ln2_b", l, 8), ("ple_b_gate", l, 8)]
        for name, l, n in vec_src:
            VCOL[name, l] = c
            c += n
        SINK = STAT[:, 0:8]
        RELB = STAT[0:33, 48:56]
        BV = PR[0:8, 1, 0:384]
        n_vec = c
        V2, c = {}, 0
        vec2_src = [("norm_mem_2", 8), ("norm_mix_pre_2", 8), ("norm_mix_post_2", 8), ("norm_ffn_pre_2", 8),
                    ("norm_ffn_post_2", 8), ("hgrn_norm_2", 2), ("pool_scale_2", 2), ("lb_logits_2", 4)]
        for name, n in vec2_src:
            V2[name] = c
            c += n
        VROW2 = VT[:, P:2 * P]
        VROW = VT[:, 0:P]
        BF = VEC[0:16, n_vec:n_vec + 1]

        def wait(eng, name, key):
            eng.wait_ge(sem[name], cnt.value(name, key))

        def done(ins, name, key):
            ins.then_inc(sem[name], 1)
            cnt.note(name, key)

        class Stream:

            def __init__(self):
                self.n = self.m = 0

            def slot(self, k, i=0, per=0):
                return (self.n + k) % 4, (self.n + k) // 4 + i * (per // 4)

            def bank(self, k, i=0, per=0):
                return (self.m + k) % 2, (self.m + k) // 2 + i * (per // 2)

        def evac_of(eng, m):
            eng.wait_ge(evac[m % 2], m // 2 + 1)

        def hi_ahead(act, st, k=0, i=0, per=0):
            s, u = st.slot(k + 3, i, per)
            if st.n + k + 3 >= total_tiles and per == 0:
                return
            act.wait_ge(loaded[s], 16 * u + 16)
            if st.n + k + 3 >= 4:
                act.wait_ge(used[s], u)
            act.activation(WH[:, s], RAW[:, s], ACT.Copy).then_inc(hi_done[s], 1)

        def lo_ahead(dve, st, k=0, i=0, per=0):
            s, u = st.slot(k + 3, i, per)
            if st.n + k + 3 >= total_tiles and per == 0:
                return
            dve.wait_ge(hi_done[s], u + 1)
            dve.tensor_tensor(WL[:, s], RAW[:, s], WH[:, s].bitcast(F32), ALU.subtract).then_inc(lo_done[s], 1)

        def lin(pe, st, tiles, rh, rl, m=P, n=T, k0=0, mo=0, i=0, per=0, perm=0, before=None):
            b, ub = st.bank(mo, i, perm)
            if st.m + mo >= 2:
                pe.wait_ge(evac[b], ub)
            kk = 0
            last = sum(tiles) - 1
            for g, nk in enumerate(tiles):
                s, u = st.slot(k0 + g, i, per)
                pe.wait_ge(lo_done[s], u + 1)
                for k in range(nk):
                    if before:
                        before(kk)
                    pe.matmul(PB[b][0:m, 0:n], WH[:, s, k, 0:m], rh[:, kk, :], start=kk == 0, stop=False)
                    pe.matmul(PB[b][0:m, 0:n], WH[:, s, k, 0:m], rl[:, kk, :], start=False, stop=False)
                    x = pe.matmul(PB[b][0:m, 0:n], WL[:, s, k, 0:m], rh[:, kk, :], start=False, stop=kk == last)
                    kk += 1
                x.then_inc(used[s], 1)

        def lin_ready(eng, st, k=0, i=0, per=0):
            s, u = st.slot(k, i, per)
            eng.wait_ge(used[s], u + 1)

        HEAD0 = {"mla": 0, "swa": 8, "fox": 16, "mem": 32, "dsa": 36}

        def keys(kind, qb):
            return {"swa": list(range(max(qb - 1, 0), qb + 1)), "mem": [0, 1]}.get(kind, list(range(qb + 1)))

        def pv_parts(kind):
            if kind == "swa":
                return [(j, q, q + 1) for q in range(TT) for j in keys(kind, q)]
            if kind == "mem":
                return [(0, 0, TT), (1, 0, TT)]
            return [(j, j, TT) for j in range(TT)]

        def operands(kind, h):
            if kind in ("dsa", "mem"):
                return operands2(kind, h)
            r = slice(h % 2 * 64, h % 2 * 64 + 64)
            if kind == "mla":
                return Q96[:, h], K96[:, h], lambda j: V4[:, j, h * 64:h * 64 + 64], 96 ** -0.5
            if kind == "swa":
                return QS[r, h // 2], K2[r, h // 4], lambda j: VS[:, j, h // 4 * 64:h // 4 * 64 + 64], 0.125
            if kind == "fox":
                pp = h // 2 % 2
                return QA[:, pp, h % 2], KA[:, pp, h % 2], lambda j: VP[:, pp, j, h % 2 * 64:h % 2 * 64 + 64], 1.0

        def score_read(n):
            return "biased" if 32 <= n < 64 else "score_free"

        def operands2(kind, h):
            r = slice(h % 2 * 64, h % 2 * 64 + 64)
            if kind == "dsa":
                return SQ_[r, h // 2], SK2[r], lambda j: SV[:, j], 0.125
            return MQ[r, h // 2], MK[r, h // 2], lambda j: MV[:, j, h * 64:h * 64 + 64], 0.125

        def pe_scores(pe, kind, h, qb):
            n = (HEAD0[kind] + h) * 4 + qb
            q, k, _, _ = operands(kind, h)
            if n >= 2:
                wait(pe, score_read(n - 2), n - 2)
            bank = PB[2 + n % 2]
            ks = keys(kind, qb)
            lo = (ks[0] - qb + 1) * P if kind == "swa" else 0
            w = len(ks) * P
            plain = kind in ("swa", "mem")
            x = pe.matmul(bank[:, lo:lo + w], q[:, qb * P:qb * P + P], k[:, ks[0] * P:ks[0] * P + w], start=True, stop=plain)
            if not plain:
                if kind == "dsa":
                    x = pe.matmul(bank[:, 0:w], ID16[:], MSK[:, qb, 0:w], start=False, stop=True)
                else:
                    x = pe.matmul(bank[:, w - P:w], ID16[:], CA16[:], start=False, stop=True)
            done(x, "scores", n)

        def pe_transposes(pe, kind, h, qb):
            n = (HEAD0[kind] + h) * 4 + qb
            ks = keys(kind, qb)
            wait(pe, "probs_n", n)
            if n >= 2:
                wait(pe, "ptev", n - 2)
            for c, _ in enumerate(ks):
                x = pe.transpose(PB[4 + n % 2][:, c * P:c * P + P], PR[:, n % 2, c * P:c * P + P], ID[:])
            done(x, "ptrans", n)

        def pe_values(pe, kind, h):
            hg = HEAD0[kind] + h
            v = operands(kind, h)[2]
            wait(pe, "ptev", hg * 4 + 3)
            if hg >= 2:
                wait(pe, "o_lo", (hg - 2) // 2)
            r = slice(h % 2 * 64, h % 2 * 64 + 64)
            parts = pv_parts(kind)
            seen = set()
            for c, (j, q0, q1) in enumerate(parts):
                first = c == 0
                if kind == "swa":
                    first = q0 not in seen
                    seen.add(q0)
                    lastp = not any(p[1] == q0 for p in parts[c + 1:])
                else:
                    lastp = c == len(parts) - 1
                x = pe.matmul(PB[6][r, q0 * P:q1 * P], v(j), PT[:, h % 2, j, q0 * P:q1 * P], start=first, stop=lastp)
            done(x, "pv", hg)

        def nothing(c):
            pass

        def pe_attend(pe, kind, heads, order0=None):
            items = [(h, qb) for h in heads for qb in range(TT)]
            pe_scores(pe, kind, *items[0])
            pe_scores(pe, kind, *items[1])
            for c, (h, qb) in enumerate(items):
                if c + 2 < len(items):
                    pe_scores(pe, kind, *items[c + 2])
                pe_transposes(pe, kind, h, qb)
                if qb == 0 and c:
                    pe_values(pe, kind, h - 1)
            pe_values(pe, kind, heads[-1])

        def dve_max(dve, kind, h, qb):
            n = (HEAD0[kind] + h) * 4 + qb
            ks = keys(kind, qb)
            w = len(ks) * P
            st = STAT[:, 8 + 4 * (n % 4):12 + 4 * (n % 4)]
            scale = operands(kind, h)[3]
            wait(dve, "scores", n)
            if n >= 4:
                wait(dve, "probs_n", n - 4)
            if kind == "swa":
                lo = (ks[0] - qb + 1) * P
                if n >= 2:
                    wait(dve, "probs_n", n - 2)
                done(dve.scalar_tensor_tensor(SW[:, n % 2, 0:w], PB[2 + n % 2][:, lo:lo + w], scale,
                                              BIAS[:, h, lo:lo + w], ALU.mult, ALU.add), "biased", n)
                wait(dve, "biased", n)
                done(dve.reduce_max(st[:, 0:1], SW[:, n % 2, 0:w], AX.X), "chain_d", ("mx", n))
                wait(dve, "chain_d", ("mx", n))
                done(dve.tensor_scalar(st[:, 1:2], st[:, 0:1], SINK[:, h:h + 1], -1.0, ALU.max, ALU.mult), "rowmax", n)
            else:
                done(dve.reduce_max(st[:, 0:1], PB[2 + n % 2][:, 0:w], AX.X), "chain_d", ("mx", n))
                wait(dve, "chain_d", ("mx", n))
                done(dve.tensor_scalar(st[:, 1:2], st[:, 0:1], -scale, None, ALU.mult), "rowmax", n)

        def act_exp(act, kind, h, qb):
            n = (HEAD0[kind] + h) * 4 + qb
            w = len(keys(kind, qb)) * P
            st = STAT[:, 8 + 4 * (n % 4):12 + 4 * (n % 4)]
            scale = operands(kind, h)[3]
            wait(act, "rowmax", n)
            if n >= 2:
                wait(act, "ptrans", n - 2)
            if kind == "swa":
                done(act.activation(PR[:, n % 2, 0:w], SW[:, n % 2, 0:w], ACT.Exp, bias=st[:, 1:2],
                                    accum_out=st[:, 2:3]), "probs", n)
                done(act.activation(st[:, 3:4], SINK[:, h:h + 1], ACT.Exp, bias=st[:, 1:2]), "sinkexp", n)
            else:
                done(act.activation(PR[:, n % 2, 0:w], PB[2 + n % 2][:, 0:w], ACT.Exp, bias=st[:, 1:2],
                                    scale=scale, accum_out=st[:, 2:3]), "score_free", n)

        def dve_normalise(dve, kind, h, qb):
            n = (HEAD0[kind] + h) * 4 + qb
            w = len(keys(kind, qb)) * P
            st = STAT[:, 8 + 4 * (n % 4):12 + 4 * (n % 4)]
            if kind == "swa":
                wait(dve, "sinkexp", n)
                done(dve.tensor_tensor(st[:, 2:3], st[:, 2:3], st[:, 3:4], ALU.add), "chain_d", ("sum", n))
                wait(dve, "chain_d", ("sum", n))
            else:
                wait(dve, "score_free", n)
            done(dve.reciprocal(st[:, 0:1], st[:, 2:3]), "chain_d", ("rec", n))
            wait(dve, "chain_d", ("rec", n))
            done(dve.tensor_scalar(PR[:, n % 2, 0:w], PR[:, n % 2, 0:w], st[:, 0:1], None, ALU.mult), "probs_n", n)

        def act_copy_transposed(act, kind, h, qb):
            hg = HEAD0[kind] + h
            n = hg * 4 + qb
            ks = keys(kind, qb)
            wait(act, "ptrans", n)
            if hg >= 2:
                wait(act, "pv", hg - 2)
            done(act.activation(PT[:, h % 2, ks[0]:ks[0] + len(ks), qb * P:qb * P + P],
                                PB[4 + n % 2][:, 0:len(ks) * P].rearrange("p (j q) -> p j q", q=P), ACT.Copy), "ptev", n)

        def out_parts(kind):
            if kind in ("dsa", "mem"):
                br = 2 if kind == "dsa" else 3
                return YH[:, br], YL[:, br]
            return (OH, OL) if kind == "fox" else (XH, XL)

        def act_out(act, kind, pair, tile):
            g = HEAD0[kind] // 2 + pair
            wait(act, "pv", 2 * g + 1)
            done(act.activation(out_parts(kind)[0][:, tile], PB[6][:], ACT.Copy), "o_hi", g)

        def dve_out(dve, kind, pair, tile):
            g = HEAD0[kind] // 2 + pair
            wait(dve, "o_hi", g)
            oh, ol = out_parts(kind)
            done(dve.tensor_tensor(ol[:, tile], PB[6][:], oh[:, tile].bitcast(F32), ALU.subtract), "o_lo", g)

        def act_attend(act, kind, heads, tile0, between=nothing):
            items = [(h, qb) for h in heads for qb in range(TT)]
            act_exp(act, kind, *items[0])
            for c, (h, qb) in enumerate(items):
                if c + 1 < len(items):
                    act_exp(act, kind, *items[c + 1])
                act_copy_transposed(act, kind, h, qb)
                if h % 2 == 0 and qb == 0 and c:
                    act_out(act, kind, h // 2 - 1, tile0 + h // 2 - 1)
                between(c)
            act_out(act, kind, heads[-1] // 2, tile0 + heads[-1] // 2)

        def dve_attend(dve, kind, heads, tile0, between=nothing):
            items = [(h, qb) for h in heads for qb in range(TT)]
            dve_max(dve, kind, *items[0])
            for c, (h, qb) in enumerate(items):
                if c + 1 < len(items):
                    dve_max(dve, kind, *items[c + 1])
                dve_normalise(dve, kind, h, qb)
                if h % 2 == 0 and qb == 1 and c > 1:
                    dve_out(dve, kind, h // 2 - 1, tile0 + h // 2 - 1)
                between(c)
            dve_out(dve, kind, heads[-1] // 2, tile0 + heads[-1] // 2)

        SW = RS[:].rearrange("p (a n) -> p a n", a=2)

        def pe_misc(pe, k, fn):
            if misc_order[k] > 0:
                wait(pe, "misc_free", misc_keys[misc_order[k] - 1])
            done(fn(), "misc", k)

        def small_bank_free(eng, k):
            if misc_order[k] > 0:
                wait(eng, "misc_free", misc_keys[misc_order[k] - 1])

        def ln_pe(pe, key):
            wait(pe, "sum8", key)
            pe_misc(pe, ("mean", key), lambda: pe.matmul(PB[7][:], ONES[:], SM[:, 1], start=True, stop=True))
            wait(pe, "misc_free", ("mean", key))
            for j in range(DT):
                wait(pe, "sqr", (key, j))
                x = pe.matmul(PB[7][:], ONES[:], X[:, j], start=j == 0, stop=j == DT - 1)
            done(x, "misc", ("var", key))

        def rsqrt_act(act, key, width, eps, n=T):
            wait(act, "misc", ("var", key))
            done(act.activation(RS[:, 0:n], PB[7][:, 0:n], ACT.Ln, bias=eps[:], scale=1.0 / width), "rs_ln", key)
            wait(act, "rs_ln", key)
            done(act.activation(RS[:, 0:n], RS[:, 0:n], ACT.Exp, scale=-0.5), "rs_exp", key)

        def rsqrt_dve(dve, key, width, eps, n=T):
            wait(dve, "misc", ("var", key))
            wait(dve, "rs_exp", key)
            done(dve.tensor_scalar(TMP[:, 0:n], PB[7][:, 0:n], 1.0 / width, eps, ALU.mult, ALU.add), "misc_free", ("var", key))
            done(dve.tensor_tensor(VT[:, 0:n], RS[:, 0:n], RS[:, 0:n], ALU.mult), "chain_d", ("n1", key))
            wait(dve, "misc_free", ("var", key))
            wait(dve, "chain_d", ("n1", key))
            done(dve.scalar_tensor_tensor(VT[:, 0:n], VT[:, 0:n], -0.5, TMP[:, 0:n], ALU.mult, ALU.mult), "chain_d", ("n2", key))
            wait(dve, "chain_d", ("n2", key))
            done(dve.scalar_tensor_tensor(RS[:, 0:n], VT[:, 0:n], 1.5, RS[:, 0:n], ALU.add, ALU.mult), "rsq", key)
            wait(dve, "rsq", key)

        def ln_act(act, key, st):
            evac_of(act, st.m - 2)
            evac_of(act, st.m - 1)
            for j in range(DT):
                wait(act, *(("cen", (key, j)) if j < DT - 1 else ("misc_free", ("mean", key))))
                done(act.activation(X[:, j], ACC[:, j], ACT.Square), "sqr", (key, j))
            rsqrt_act(act, key, D, EPS5)
            for j in range(DT):
                wait(act, "ln_t", (key, j))
                done(act.activation(XH[:, j], X[:, j], ACT.Copy), "x_hi", (key, j))

        def ln_dve(dve, key, g, b):
            evac_of(dve, M_LN[key] + DT - 1)
            wait(dve, "sum7", (key, DT - 2))
            done(dve.tensor_tensor(SM[:, 1], SM[:, 0], ACC[:, DT - 1], ALU.add), "sum8", key)
            wait(dve, "misc", ("mean", key))
            for j in range(DT):
                done(dve.scalar_tensor_tensor(ACC[:, j], PB[7][:], -1.0 / D, ACC[:, j], ALU.mult, ALU.add),
                     *(("cen", (key, j)) if j < DT - 1 else ("misc_free", ("mean", key))))
            rsqrt_dve(dve, key, D, 1e-5)
            wait(dve, "rsq", key)
            for j in range(DT + 1):
                if j < DT:
                    done(dve.scalar_tensor_tensor(ACC[:, j], ACC[:, j], VEC[:, g + j:g + j + 1], RS[:], ALU.mult, ALU.mult), "norm", (key, j))
                    wait(dve, "norm", (key, j))
                    done(dve.tensor_scalar(X[:, j], ACC[:, j], VEC[:, b + j:b + j + 1], None, ALU.add), "ln_t", (key, j))
                if j > 0:
                    wait(dve, "x_hi", (key, j - 1))
                    done(dve.tensor_tensor(XL[:, j - 1], X[:, j - 1], XH[:, j - 1].bitcast(F32), ALU.subtract), "x_lo", (key, j - 1))

        misc_keys = ["vec", "vec2", ("var", "cq"), ("var", "ckv"), "kswap", "vs", "bandv",
                     *[("qswap", h) for h in range(8)], *[("bandt", k) for k in range(4)], *[("v4", j) for j in range(4)],
                     ("mean", "ln1_0"), ("var", "ln1_0"), ("mean", "ln2_0"), ("var", "ln2_0"),
                     *[("vp", j) for j in range(8)],
                     ("mean", "ln1_1"), ("var", "ln1_1"), ("mean", "ln2_1"), ("var", "ln2_1"),
                     ("var", "mem"), ("mv", 0), ("mv", 1), ("var", "mixpre"), ("pw", 0), ("pw", 1), "iwt", "svt",
                     ("hv", 0), ("hv", 1), ("var", "hg0"), ("var", "hg1"), ("var", "mixpost"), ("var", "ffnpre"),
                     ("var", "ffnpost")]
        misc_order = {k: c for c, k in enumerate(misc_keys)}
        LAYERS = 2

        total_tiles = 12 + 16 + 8 + 64 + 16
        total_tiles += 1 + 24 + 8 + 64 + 16

        N_RANK = total_tiles + 4 + 12
        total_tiles += 4 + 24 + 64 + 8 + sum(2 * n + 16 for n in HID)
        BRANCHES = (3, 1, 2, 0)
        SLOT = (0, 4, 7, 9)
        M_MQ = 0
        M_OUT = DT + 12 + 16 + 8 + 48 + 2 + 16
        M_OUT += 1 + 24 + 8 + 48 + 2 + 16
        M_MQ = M_OUT + DT + 4
        M_OUT += DT + 4 + 24 + 64 + 8 + sum(2 * n + 8 for n in HID)

        M_LN = {"ln1_0": DT + 28, "ln2_0": DT + 78, "ln1_1": DT + 127, "ln2_1": DT + 177}

        def wview(name, l=0):
            return t[name][l].rearrange("(k p) n -> p k n", p=P)

        n_small = 16 * (3 + len(vec_src) + len(vec2_src))
        HP = 2
        block = ctx.enter_context(nc.Block())

        @block.sync
        def _(sp):
            st = Stream()

            def load(src, nk, m, k=0, i=0, per=0):
                s, u = st.slot(k, i, per)
                if st.n + k >= 4:
                    sp.wait_ge(lo_done[s], u)
                sp.dma_start(RAW[:, s, 0:nk, 0:m], src).then_inc(loaded[s], 16)

            def load_loop(view, groups, outs, k_first=0):
                seq = len(groups)
                per = 12 if seq == 3 else 4
                iters = outs * seq // per
                with sp.Fori(0, iters) as i:
                    for k in range(per):
                        o, g = divmod(k, seq)
                        k0 = k_first + sum(groups[:g])
                        load(view[:, k0:k0 + groups[g], bass.ds(i * (per // seq * P) + o * P, P)], groups[g], P, k, i, per)
                st.n += per * iters

            def loadn(src, nk, m):
                load(src, nk, m)
                st.n += 1

            def second_loads():
                W = wview("w_mem_kv_2")
                for c in range(4):
                    loadn(W[:, :, c * P:c * P + P], 8, P)
                wait(sp, "x_new", (1, DT - 1))
                for k in range(2):
                    sp.dma_start(MIN[:, k], t["mem_2"][0, k * P:k * P + P, :]).then_inc(sem["mem_in"], 16)
                sp.dma_start(CHK[:], t["tab_a"][:, C_CHUNK:C_CHUNK + P]).then_inc(sem["mem_in"], 16)
                W = wview("w_in_2")
                a = [2760, 2888, 1536, 1664, 2176, 2304, 2432, 2560, 2688, 2048, 1792, 1920]
                b = [512 + c * P for c in range(4)] + [c * P for c in range(4)] + [1024, 1152, 1280, 1408]
                for c in a[:3]:
                    loadn(W[:, :, c:c + P], 8, P)
                wait(sp, "rn", ("mixpre", DT - 1))
                sp.dma_start(CNT[:], t["tab_b"][:, C_CNT:C_CNT + 2 * T].rearrange("p (a n) -> p a n", a=2)).then_inc(sem["pw_in"], 16)
                for j in range(2):
                    sp.dma_start(PW[:, j], t["pool_w_2"][0, 2 * j:2 * j + 2].rearrange("e c d -> (e c) d")).then_inc(sem["pw_in"], 16)
                for c in a[3:] + b:
                    loadn(W[:, :, c:c + P], 8, P)
                wg, wb = t["w_gate_2"], t["w_branch_2"]
                views = [(wg[0, br].rearrange("(k p) n -> p k n", p=P), wb[0, br].rearrange("(k p) n -> p k n", p=P)) for br in BRANCHES]

                def four(g, w, i, per):
                    for k in range(4):
                        v, nk = ((g, 8), (w, 2))[k % 2]
                        load(v[:, :, bass.ds(i * 2 * P + k // 2 * P, P)], nk, P, k, i, per)
                four(*views[0], 0, 4)
                wait(sp, "scores", 159)
                wait(sp, "topk", "mask")
                sp.dma_start(LMASK[:], t["tab_b"][:, 0:8 * P].rearrange("p (l n) -> p l n", n=P)).then_inc(sem["tabb_in"], 16)
                sp.dma_start(BONE[:], t["tab_b"][:, C_BONE:C_BONE + P]).then_inc(sem["tabb_in"], 16)
                for n, (g, w) in enumerate(views):
                    with sp.Fori(0 if n else 1, 4) as i:
                        four(g, w, i, 4)
                    st.n += 16
                load_loop(wview("w_out_2"), [8], 8)
                W = wview("w_ffn_gate_up_2")
                h0 = 0
                for n in HID:
                    with sp.Fori(0, n // 2) as i:
                        for k in range(4):
                            load(W[:, :, bass.ds(i * 2 * P + (k // 2 * P + k % 2 * DFF2 + h0 * P), P)], 8, P, k, i, 4)
                    st.n += 2 * n
                    load_loop(wview("w_ffn_down_2"), [8, n - 8], 8, k_first=h0)
                    h0 += n

            sp.dma_start(ID[:], t["tab_a"][:, C_ID:C_ID + P]).then_inc(sem["const_in"], 16)
            sp.dma_start(PR[:, 0, 0:256], t["tab_a"][:, C_CAUS:C_CAUS + 256]).then_inc(sem["const_in"], 16)
            for k in range(TT):
                sp.dma_start(XIN[:, k], t["x"][0, k * P:k * P + P, :]).then_inc(sem["x_in"], 16)
            wait(sp, "zeroed", "raw")
            W = wview("ev_w_in")
            cols = [(c * P, P) for c in range(5)] + [(640, 32)] + [(672 + c * P, P) for c in range(4)] + [(1184, P), (1312, P)]
            for c, m in cols[:4]:
                loadn(W[:, :, c:c + m], 8, m)
            wait(sp, "zeroed", "relb")
            wait(sp, "zeroed", "vrow")
            sp.dma_start(RELB[0:32, :], t["rel_bias"]).then_inc(sem["relb_in"], 16)
            sp.dma_start(CST[:], t["tab_a"][:, C_ANTI:C_A]).then_inc(sem["small_in"], 16)
            for name, l, n in vec_src:
                sp.dma_start(VROW[VCOL[name, l]:VCOL[name, l] + n, :], t[name][l].rearrange("(k p) -> k p", p=P)).then_inc(sem["small_in"], 16)
            for name, n in vec2_src:
                sp.dma_start(VROW2[V2[name]:V2[name] + n, :], t[name][0].rearrange("(k p) -> k p", p=P)).then_inc(sem["small_in"], 16)
            sp.dma_start(SINK, t["ev_sinks"][0:1, :].to_broadcast([P, 8])).then_inc(sem["small_in"], 16)
            sp.dma_start(VROW[n_vec:n_vec + 1, 0:16], t["od_b_f"]).then_inc(sem["small_in"], 16)
            for c, m in cols[4:]:
                loadn(W[:, :, c:c + m], 8, m)
            W = t["ev_w_uq"][0].rearrange("(k p) (h n) -> p k h n", p=P, n=96)
            for h in range(4):
                loadn(W[:, :, h], 3, 96)
            wait(sp, "misc_free", "bandv")
            sp.dma_start(band_dram, BV).then_inc(sem["band_out"], 16)
            sp.wait_ge(sem["band_out"], 16)
            sp.dma_start(BAND[:], bass.AP(band_dram.tensor, 0, [[1, P], [384, 8], [1, 256]])).then_inc(sem["band_in"], 16)
            for h in range(4, 8):
                loadn(W[:, :, h], 3, 96)
            W = wview("ev_w_ukv")
            for h in range(8):
                loadn(W[:, :, h * P:h * P + P], 2, P)

            def mlp(l):
                for half in range(2):
                    if half:
                        wait(sp, "x_lo", (f"ln1_{l}", DT - 1))
                        for k in range(TT):
                            sp.dma_start(PIN[:, k], t["p"][l, 0, k * P:k * P + P, :]).then_inc(sem["p_in"], 16)
                    load_loop(wview("w_up", l)[:, :, half * 2048:half * 2048 + 2048], [8], 16)
                    load_loop(wview("w_down", l), [8, 8], 8, k_first=half * 16)

            def ple(l):
                wg, wp = wview("ple_w_gate", l), wview("ple_w_proj", l)

                def four(i, per):
                    for k in range(4):
                        v, nk = ((wg, 8), (wp, 2))[k % 2]
                        load(v[:, :, bass.ds(i * 2 * P + k // 2 * P, P)], nk, P, k, i, per)
                with sp.Fori(0, 4) as i:
                    four(i, 4)
                st.n += 16

            load_loop(wview("ev_w_out"), [8], 8)
            mlp(0)
            ple(0)
            W = wview("od_w_in")
            loadn(W[:, :, 3072:3088], 8, 16)
            for j in range(8):
                for c in range(3):
                    loadn(W[:, :, c * D + j * P:c * D + j * P + P], 8, P)
                if j == 0:
                    wait(sp, "zeroed", "ones_q")
                    wait(sp, "fox_c", 1)
                if j >= 2:
                    wait(sp, "scores", (16 + 2 * (j - 2) + 1) * 4 + 3)
                for e in range(2):
                    h = 2 * j + e
                    into = sem["aug_in" if j % 2 == 0 else "aug2_in"]
                    sp.dma_start(QA[65:66, j % 2, e], FZ[h:h + 1, 3]).then_inc(into, 16)
                    sp.dma_start(KA[64:65, j % 2, e], FZ[h:h + 1, 4]).then_inc(into, 16)
            load_loop(wview("od_w_out"), [8], 8)
            mlp(1)
            ple(1)
            second_loads()
            for g in range(2):
                for k in range(TT):
                    evac_of(sp, M_OUT + TT * g + k)
                    sp.dma_start(t["y"][0, k * P:k * P + P, g * T:g * T + T], OUTT[:, g, k]).then_inc(sem["y_out"], 16)
            sp.wait_ge(sem["y_out"], 16 * 2 * TT)

        @block.gpsimd
        def _(pool):
            done(pool.memset(RAW[:], 0.0), "zeroed", "raw")
            done(pool.memset(VT[:, 0:2 * P], 0.0), "zeroed", "vrow")
            done(pool.memset(ONES[:], 1.0), "zeroed", "ones")
            done(pool.memset(EPS5[:], 1e-5), "zeroed", "eps")
            done(pool.memset(STAT[0:64, 48:56], NEG), "zeroed", "relb")
            done(pool.memset(KR[0:64, :], 0.0), "zeroed", "kr")

            def sums(key):
                m = M_LN[key]
                evac_of(pool, m)
                for j in range(1, DT - 1):
                    evac_of(pool, m + j)
                    if j > 1:
                        wait(pool, "sum7", (key, j - 1))
                    done(pool.tensor_tensor(SM[:, 0], SM[:, 0] if j > 1 else ACC[:, 0], ACC[:, j], ALU.add), "sum7", (key, j))
            wait(pool, "zeroed", "kr")
            wait(pool, "kr", "rot")
            wait(pool, "misc_free", ("bandt", 3))
            for h in range(8):
                x = pool.tensor_copy(K96[64:96, h], KR[64:96, :])
            done(x, "chain_p", "krope")
            sums("ln1_0")
            sums("ln2_0")
            wait(pool, "x_lo", ("ple0", DT - 1))
            done(pool.memset(QA[64:66, :, :, :], 1.0), "zeroed", "ones_k")
            done(pool.memset(KA[64:66, :, :, :], 1.0), "zeroed", "ones_q")
            sums("ln1_1")
            sums("ln2_1")

            wait(pool, "x_new", (1, DT - 1))
            done(pool.memset(EPS6[:], 1e-6), "zeroed", "eps6")
            wait(pool, "rn", ("mixpre", DT - 1))
            done(pool.memset(PZ[:, :, 0:16], 0.0), "zeroed", "pz")
            done(pool.memset(TMP[:], 1.0), "zeroed", "tmp")
            wait(pool, "zeroed", "tmp")
            done(pool.memset(TMP[:].rearrange("p (c n) -> p c n", n=64)[:, :, 0:1], 0.0), "zeroed", "restart")
            st = Stream()
            st.n = N_RANK
            for c in range(12):
                lo_ahead(pool, st)
                st.n += 1
            wait(pool, "ptev", 159)
            wait(pool, "o_lo", 19)
            done(pool.memset(ATT[:], 0.0), "zeroed", "att")

        @block.tensor
        def _(pe):
            st = Stream()

            def turn(key, src, n_in):
                def go():
                    for k in range(n_in):
                        x = pe.transpose(PB[7][:, k * P:k * P + P], src[:, k * P:k * P + P], ID[:])
                    return x
                pe_misc(pe, key, go)

            def turn_in(key, src):
                b, ub = st.bank(0)
                if st.m >= 2:
                    pe.wait_ge(evac[b], ub)
                for k in range(TT):
                    x = pe.transpose(PB[b][:, k * P:k * P + P], src(k), ID[:])
                done(x, "xt", key)
                st.m += 1

            pe.wait_ge(sem["const_in"], 32)
            pe.wait_ge(sem["x_in"], 16 * TT)
            for j in range(DT):
                turn_in(j, lambda k: XIN[:, k, j * P:j * P + P])

            def lin1(nk, rh, rl, m=P, before=None):
                lin(pe, st, [nk], rh, rl, m, before=before)
                st.n += 1
                st.m += 1

            def x_before(key):
                return lambda k: wait(pe, "x_lo", (key, k))

            def squares(key, js):
                def go():
                    for j in js:
                        wait(pe, "sq", j)
                        x = pe.matmul(PB[7][:], ONES[:], PT[:, j // 4, j % 4], start=j == js[0], stop=j == js[-1])
                    return x
                pe_misc(pe, ("var", key), go)

            def sum_squares(key, src, n, width=T, ones=None):
                def go():
                    for j in range(n):
                        wait(pe, "sq2", (key, j))
                        x = pe.matmul(PB[7][:, 0:width], (ONES if ones is None else ones)[:], src[:, j], start=j == 0, stop=j == n - 1)
                    return x
                pe_misc(pe, ("var", key), go)

            def second_pe():
                pe.wait_ge(sem["mem_in"], 48)
                for j in range(DT):
                    b, ub = st.bank(0)
                    pe.wait_ge(evac[b], ub)
                    for k in range(2):
                        x = pe.transpose(PB[b][:, k * P:k * P + P], MIN[:, k, j * P:j * P + P], ID[:])
                    done(x, "xt", ("mem", j))
                    st.m += 1
                sum_squares("mem", SQM, DT, NMEM)
                for c in range(4):
                    lin(pe, st, [8], MH, ML, n=NMEM, before=(lambda k: wait(pe, "r_lo", ("mem", k))) if c == 0 else None)
                    st.n += 1
                    st.m += 1
                    if c >= 2:
                        evac_of(pe, st.m - 1)
                        turn(("mv", c - 2), VT, 2)
                sum_squares("mixpre", SQX, DT)
                lin1(8, XH, XL, before=lambda k: wait(pe, "r_lo", ("mixpre", k)))
                for c in range(7):
                    lin1(8, XH, XL)
                pe.wait_ge(sem["pw_in"], 48)
                for j in range(2):
                    def go(j=j):
                        for e in range(2):
                            r = slice(e * 64, e * 64 + 64)
                            x = pe.matmul(PB[7][r], PW[r, j], PO[r, j], start=True, stop=True)
                        return x
                    wait(pe, "pooled", j)
                    pe_misc(pe, ("pw", j), go)
                for key in ("iwt", "svt"):
                    lin1(8, XH, XL)
                    evac_of(pe, st.m - 1)
                    turn(key, VT, 4)
                lin1(8, XH, XL)
                lin1(8, XH, XL)
                evac_of(pe, M_MQ + 1)
                evac_of(pe, M_MQ)
                wait(pe, "misc_free", ("mv", 1))
                pe_attend(pe, "mem", range(4), order0=HEAD0["mem"])
                evac_of(pe, M_MQ + 8)
                evac_of(pe, M_MQ + 7)
                wait(pe, "score_free", 143)
                wait(pe, "score_free", 142)
                for r in range(24):
                    qb, ih = r // 8 + 1, r % 8
                    rr = slice(ih % 2 * 64, ih % 2 * 64 + 64)
                    if r >= 2:
                        wait(pe, "ixr", r - 2)
                    x = pe.matmul(PB[2 + r % 2][:, 0:(qb + 1) * P], IQ[rr, ih // 2, qb * P:qb * P + P], IK2[rr, 0:(qb + 1) * P], start=True, stop=True)
                    done(x, "ix", r)
                for c in range(12):
                    lin1(8, XH, XL)
                    if c in (8, 9):
                        evac_of(pe, st.m - 1)
                        turn(("hv", c - 8), VT, 4)
                wait(pe, "topk", "mask")
                wait(pe, "misc_free", "svt")
                wait(pe, "ixr", 23)
                pe_attend(pe, "dsa", range(4), order0=HEAD0["dsa"])
                pe.wait_ge(sem["tabb_in"], 32)
                wait(pe, "o_lo", 19)
                wait(pe, "ptev", 159)
                wait(pe, "score_free", 159)
                q = 0

                def room():
                    if q >= 4:
                        wait(pe, "hg_read", q - 4)
                for lv in range(8):
                    wait(pe, "hg_x", (lv, 1)) if lv < 7 else wait(pe, "hg_small", "qk")
                    for a in range(TT):
                        room()
                        for h in range(4):
                            sl = slice(a * P, a * P + P)
                            l_, r_ = (XX[:, h, sl], XX[:, h, sl]) if lv < 7 else (KK[:, h, sl], QQ[:, h, sl])
                            x = pe.matmul(PB[2 + q % 4][:, h * P:h * P + P], l_, r_, start=True, stop=True)
                        done(x, "hg_prod", q)
                        q += 1
                wait(pe, "hg_x", (7, 1))
                for pr in range(2):
                    room()
                    for h in range(4):
                        x = pe.matmul(PB[2 + q % 4][:, h * P:h * P + P], XX[:, h, 2 * pr * P:(2 * pr + 1) * P],
                                      XX[:, h, (2 * pr + 1) * P:(2 * pr + 2) * P], start=True, stop=True)
                    done(x, "hg_prod", q)
                    q += 1
                wait(pe, "hg_x", (8, 1))
                for h in range(4):
                    room()
                    for a in range(2):
                        x = pe.matmul(PB[2 + q % 4][:, a * 256:a * 256 + 256], XX[:, h, a * P:a * P + P], XX[:, h, 2 * P:4 * P], start=True, stop=True)
                    done(x, "hg_prod", q)
                    q += 1
                wait(pe, "hg_read", q - 1)
                wait(pe, "misc_free", ("hv", 1))
                for pr in range(2):
                    for e in range(2):
                        h = 2 * pr + e
                        for a in range(TT):
                            x = pe.matmul(PB[6 - 4 * pr][e * 64:e * 64 + 64, a * P:T], HV[:, a, h * 64:h * 64 + 64],
                                          ATT[:, h, SLOT[a]:SLOT[a] + TT - a, :], start=a == 0, stop=a == TT - 1)
                    done(x, "hg_o", pr)
                for pr in range(2):
                    def go(pr=pr):
                        wait(pe, "sq2", ("hg", pr))
                        return pe.matmul(PB[7][:], BONE[:], OS[:, pr], start=True, stop=True)
                    pe_misc(pe, ("var", f"hg{pr}"), go)
                for n, br in enumerate(BRANCHES):
                    if br == 0:
                        wait(pe, "y_lo", ("hg", 1))
                    with pe.Fori(0, 4) as i:
                        for o in range(2):
                            lin(pe, st, [8], XH, XL, k0=2 * o, mo=2 * o, i=i, per=4, perm=4)
                            lin(pe, st, [2], YH[:, br], YL[:, br], k0=2 * o + 1, mo=2 * o + 1, i=i, per=4, perm=4)
                    st.n += 16
                    st.m += 16
                lin_loop([8], 8, XH, XL, first=lambda k: wait(pe, "r_lo", ("merged", k)))
                sum_squares("mixpost", SQX, DT)
                sum_squares("ffnpre", SQX, DT)
                for c, n in enumerate(HID):
                    hb = sum(HID[:c])
                    for o in range(2):
                        for e in range(2):
                            lin1(8, XH, XL, before=(lambda k: wait(pe, "r_lo", ("ffnpre", k))) if c == o == e == 0 else None)
                    with pe.Fori(1, n // 2) as i:
                        for k in range(4):
                            lin(pe, st, [8], XH, XL, k0=k - 4, mo=k - 4, i=i, per=4, perm=4)
                    st.n += 2 * n - 4
                    st.m += 2 * n - 4
                    lin_loop([8, n - 8], 8, H2, L2, first=lambda k: pe.wait_ge(sem["hsp"], HP + hb + k + 1))
                sum_squares("ffnpost", SQX, DT)

            lin1(8, XH, XL, before=x_before("in"))
            for c in range(4):
                lin1(8, XH, XL)
            wait(pe, "zeroed", "ones")
            pe.wait_ge(sem["small_in"], n_small)
            pe_misc(pe, "vec", lambda: pe.transpose(PB[7][:, 0:P], VROW, ID[:]))
            pe_misc(pe, "vec2", lambda: pe.transpose(PB[7][:, 0:P], VROW2, ID[:]))
            squares("cq", range(3))
            squares("ckv", range(3, 5))
            lin1(8, XH, XL, 32)
            lin1(8, XH, XL)
            evac_of(pe, DT + 5)
            pe.wait_ge(sem["small_in"], n_small)
            wait(pe, "zeroed", "kr")
            SWAPc = CST[0:96, C_SWAP - C_ANTI:C_SWAP - C_ANTI + 96]
            pe_misc(pe, "kswap", lambda: pe.matmul(PB[7][0:96, :], SWAPc, KR[:], start=True, stop=True))
            for c in range(4):
                lin1(8, XH, XL)
            lin1(8, XH, XL)
            evac_of(pe, st.m - 1)
            turn("vs", VT, 4)
            pe.wait_ge(sem["relb_in"], 16)
            pe_misc(pe, "bandv", lambda: pe.matmul(PB[7][0:8, 0:384], RELB, CST[0:33, C_OH - C_ANTI:C_OH - C_ANTI + 384], start=True, stop=True))
            def qswap(h):
                evac_of(pe, DT + 12 + h)
                pe_misc(pe, ("qswap", h), lambda: pe.matmul(PB[7][0:96, :], SWAPc, Q96[:, h], start=True, stop=True))
            wait(pe, "n_lo", 4)
            for h in range(8):
                lin1(3, CQH, CQL, 96)
                if h:
                    qswap(h - 1)
            qswap(7)
            pe.wait_ge(sem["band_in"], 16)
            for k in range(4):
                pe_misc(pe, ("bandt", k), lambda: pe.matmul(PB[7][:], CST[:, 0:P], BAND[:, 2 * k:2 * k + 2, :], start=True, stop=True))
            for h in range(8):
                lin1(2, CKH, CKL)
                if h % 2:
                    evac_of(pe, st.m - 2)
                    evac_of(pe, st.m - 1)
                    turn(("v4", h // 2), VT, 4)
            wait(pe, "misc_free", ("v4", 3))
            wait(pe, "chain_p", "krope")
            wait(pe, "qrope", ("rot", 7))
            wait(pe, "ident", 0)
            pe_attend(pe, "mla", range(8))
            pe_attend(pe, "swa", range(8))

            def lin_loop(groups, outs, rh, rl, first=None):
                seq = len(groups)
                per = 12 if seq == 3 else 4
                po = per // seq
                peeled = 0
                if first:
                    for o in range(po):
                        lin(pe, st, groups, rh, rl, before=first if o == 0 else None)
                        st.n += seq
                        st.m += 1
                    peeled = po
                iters = (outs - peeled) // po
                assert po % 2 == 0
                with pe.Fori(0, iters) as i:
                    for o in range(po):
                        lin(pe, st, groups, rh, rl, k0=o * seq, mo=o, i=i, per=per, perm=po)
                st.n += per * iters
                st.m += po * iters

            def mlp(l):
                for half in range(2):
                    if half:
                        pe.wait_ge(sem["p_in"], 16 * TT * (l + 1))
                        for j in range(2):
                            turn_in(("p", l, j), lambda k: PIN[:, k, j * P:j * P + P])
                    hb = HP + (2 * l + half) * 16
                    lin_loop([8], 16, XH, XL, first=x_before(f"ln1_{l}") if half == 0 else None)
                    lin_loop([8, 8], 8, HH, HL, first=lambda k: pe.wait_ge(sem["h_lo"], hb + k + 1))

            def ple(l):
                for o in range(2):
                    lin1(8, XH, XL, before=None if o else x_before(f"ln2_{l}"))
                    lin1(2, PTH, PTL)
                with pe.Fori(1, 4) as i:
                    for o in range(2):
                        lin(pe, st, [8], XH, XL, k0=2 * o - 4, mo=2 * o - 4, i=i, per=4, perm=4)
                        lin(pe, st, [2], PTH, PTL, k0=2 * o - 3, mo=2 * o - 3, i=i, per=4, perm=4)
                st.n += 12
                st.m += 12

            wait(pe, "o_lo", 7)
            lin_loop([8], 8, XH, XL)
            ln_pe(pe, "ln1_0")
            mlp(0)
            ln_pe(pe, "ln2_0")
            ple(0)
            lin1(8, XH, XL, 16, before=x_before("ple0"))

            def project(j):
                for c in range(3):
                    lin1(8, XH, XL)
                evac_of(pe, st.m - 2)
                evac_of(pe, st.m - 1)
                turn(("vp", j), VT, 4)
            project(0)
            for j in range(8):
                if j < 7:
                    project(j + 1)
                pe.wait_ge(sem["aug_in" if j % 2 == 0 else "aug2_in"], 64 * (j // 2 + 1))
                wait(pe, "misc_free", ("vp", j))
                pe_attend(pe, "fox", [2 * j, 2 * j + 1])
            wait(pe, "o_lo", 15)
            lin_loop([8], 8, OH, OL)
            ln_pe(pe, "ln1_1")
            mlp(1)
            ln_pe(pe, "ln2_1")
            ple(1)
            second_pe()
            for g in range(2):
                j = 4 * g + 3
                wait(pe, "hx", ("ffnpost", j))
                for k in range(TT):
                    b, ub = st.bank(0)
                    pe.wait_ge(evac[b], ub)
                    for j in range(4):
                        x = pe.transpose(PB[b][:, j * P:j * P + P], X[:, 4 * g + j, k * P:k * P + P], ID[:])
                    done(x, "out_t", (k, g))
                    st.m += 1

        @block.scalar
        def _(act):
            st = Stream()
            act.wait_ge(sem["const_in"], 32)
            done(act.activation(ID16[:], ID[:], ACT.Copy), "chain_a", "id16")
            done(act.activation(CA16[:], PR[:, 0, 0:P], ACT.Copy), "ident", 0)
            wait(act, "zeroed", "eps")
            for k in range(-3, 0):
                hi_ahead(act, st, k)
            for j in range(DT):
                b, ub = st.bank(0)
                wait(act, "xt", j)
                done(act.activation(XH[:, j], PB[b][:], ACT.Copy), "x_hi", ("in", j))
                st.m += 1

            def step():
                hi_ahead(act, st)
                lin_ready(act, st)

            def nxt():
                st.n += 1
                st.m += 1

            def skip():
                hi_ahead(act, st)
                nxt()

            for c in range(5):
                hi_ahead(act, st)
                evac_of(act, st.m)
                done(act.activation(PT[:, c // 4, c % 4], ACC[:, c], ACT.Square), "sq", c)
                nxt()
            act.wait_ge(sem["small_in"], n_small)
            skip()
            rsqrt_act(act, "cq", 384, EPS5)
            for j in range(3):
                wait(act, "norm", ("c", j))
                done(act.activation(CQH[:, j], ACC[:, j], ACT.Copy), "n_hi", j)
            wait(act, "n_lo", 2)
            rsqrt_act(act, "ckv", 256, EPS5)
            for j in range(3, 5):
                wait(act, "norm", ("c", j))
                done(act.activation(CKH[:, j - 3], ACC[:, j], ACT.Copy), "n_hi", j)
            for c in range(4):
                step()
                b, ub = st.bank(0)
                act.activation(QS[:, c], PB[b][:], ACT.Copy).then_inc(evac[b], 1)
                nxt()
            skip()
            step()
            b, ub = st.bank(0)
            act.activation(VT[:], PB[b][:], ACT.Copy).then_inc(evac[b], 1)
            nxt()
            for h in range(8):
                skip()
            for h in range(8):
                step()
                b, ub = st.bank(0)
                act.activation(K96[0:64, h], PB[b][0:64], ACT.Copy)
                if h % 2 == 0:
                    wait(act, "misc", ("v4", h // 2 - 1) if h else "vs")
                act.activation(VT[h % 2 * 64:h % 2 * 64 + 64, :], PB[b][64:128], ACT.Copy).then_inc(evac[b], 1)
                nxt()
            act_attend(act, "mla", range(8), 0)
            act_attend(act, "swa", range(8), 4)

            def split_loop(tiles, outs):
                with act.Fori(0, tiles // 4) as i:
                    for k in range(4):
                        hi_ahead(act, st, k, i, 4)
                st.n += tiles
                st.m += outs

            def mlp(l):
                for half in range(2):
                    for j in range(2 * half):
                        b, ub = st.bank(0)
                        wait(act, "xt", ("p", l, j))
                        done(act.activation(PTH[:, j], PB[b][:], ACT.Copy), "pt_hi", (l, j))
                        st.m += 1
                    hb = (2 * l + half) * 16
                    with act.Fori(0, 4) as i:
                        for k in range(4):
                            hi_ahead(act, st, k, i, 4)
                            b, ub = st.bank(k, i, 4)
                            act.wait_ge(evac[b], ub + 1)
                            act.wait_ge(sem["h_lo"], i * 4 + (HP + hb + k - 1))
                            act.activation(HS[:, k % 2], HR[:, k % 2], ACT.Square).then_inc(sem["h_sq"], 1)
                            act.wait_ge(sem["h_sq"], i * 4 + (hb + k + 1))
                            act.activation(HH[:, bass.ds(i * 4 + k, 1), :], HS[:, k % 2:k % 2 + 1], ACT.Copy).then_inc(sem["h_hi"], 1)
                    st.n += 16
                    st.m += 16
                    split_loop(16, 8)

            def ple(l):
                for o in range(8):
                    step()
                    b, ub = st.bank(0)
                    if o >= 2:
                        evac_of(act, st.m - 3)
                    act.activation(GT[:, o % 2], PB[b][:], ACT.Tanh, bias=HB[:, l * 8 + o:l * 8 + o + 1], scale=0.5).then_inc(evac[b], 1)
                    nxt()
                    skip()
                if l < LAYERS - 1:
                    s, u = st.slot(-1)
                    act.wait_ge(used[s], u + 1)
                    for j in range(DT):
                        wait(act, "x_new", (l, j))
                        done(act.activation(XH[:, j], X[:, j], ACT.Copy), "x_hi", (f"ple{l}", j))

            def copy_out(dst, parts=None):
                step()
                b, ub = st.bank(0)
                for d, rows in (parts or [(dst, slice(0, P))]):
                    x = act.activation(d, PB[b][rows, 0:d.shape[-1]], ACT.Copy)
                x.then_inc(evac[b], 1)
                nxt()

            def squares(key, src, dst):
                for j in range(DT):
                    done(act.activation(dst[:, j], src[:, j], ACT.Square), "sq2", (key, j))

            def highs(key, src, dst):
                for j in range(DT):
                    wait(act, "rn", (key, j))
                    done(act.activation(dst[:, j], src[:, j], ACT.Copy), "r_hi", (key, j))

            def second_act():
                for j in range(DT):
                    evac_of(act, st.m)
                    done(act.activation(SQM[:, j], MT[:, j], ACT.Square), "sq2", ("mem", j))
                    st.m += 1
                wait(act, "zeroed", "eps6")
                rsqrt_act(act, "mem", D, EPS6, NMEM)
                highs("mem", MT, MH)
                for c in range(2):
                    copy_out(MK[:, c])
                copy_out(VT[:, 0:NMEM])
                wait(act, "misc", ("mv", 0))
                copy_out(VT[:, 0:NMEM])
                squares("mixpre", X, SQX)
                rsqrt_act(act, "mixpre", D, EPS6)
                highs("mixpre", ACC, XH)
                for c in range(2):
                    copy_out(MQ[:, c])
                for c in range(2):
                    copy_out(PZ[:, c, 16:528])
                for c in range(4):
                    copy_out(IQ[:, c])
                for j in range(2):
                    wait(act, "misc", ("pw", j))
                    g = V2["pool_scale_2"] + j
                    done(act.activation(YH[:, 1, j], PB[7][:], ACT.Copy, scale=VEC2[:, g:g + 1]), "y_hi", ("pool", j))
                copy_out(None, [(VT[:], slice(0, P)), (IK2[0:64], slice(0, 64)), (IK2[64:128], slice(0, 64))])
                wait(act, "misc", "iwt")
                copy_out(None, [(VT[:], slice(0, P)), (SK2[0:64], slice(0, 64)), (SK2[64:128], slice(0, 64))])
                wait(act, "pooled", 1)
                for c in range(2):
                    copy_out(SQ_[:, c])
                act_attend(act, "mem", range(4), 0)
                for r in range(24):
                    w = (r // 8 + 2) * P
                    wait(act, "ix", r)
                    wait(act, *(("ixs", r - 2) if r >= 2 else ("ptrans", 143)))
                    done(act.activation(PR[:, r % 2, 0:w], PB[2 + r % 2][:, 0:w], ACT.Relu, scale=0.125), "ixr", r)
                for c in range(8):
                    copy_out(ACC[:, c])
                wait(act, "misc", "svt")
                copy_out(VT[:])
                wait(act, "misc", ("hv", 0))
                copy_out(VT[:])
                for c in range(2):
                    copy_out(HG[:, c])
                done(act.activation(ACC[:, 0:4], ACC[:, 0:4], ACT.Exp, scale=-1.0), "hg_e", "gate")
                wait(act, "hg_small", "lb0")
                done(act.activation(LBV[:, 1], LBV[:, 0], ACT.Exp), "hg_e", "lb")

                def hgrn_logs(c):
                    if c == 9:
                        wait(act, "hg_small", "split")
                        done(act.activation(ACC[:, 0:4], ACC[:, 0:4], ACT.Ln), "hg_e", "ln1")
                        done(act.activation(FC[:], FC[:], ACT.Ln), "hg_e", "ln2")
                    if c == 14:
                        wait(act, "hg_small", "scan")
                        done(act.activation(ACC[:, 0:4], ACC[:, 4:8], ACT.Tanh, scale=0.5), "hg_e", "tanh")
                act_attend(act, "dsa", range(4), 0, hgrn_logs)
                for lv in range(9):
                    wait(act, "hg_d", (lv, 1))
                    done(act.activation(EE[:], EE[:], ACT.Exp), "hg_e", lv)
                for pr in range(2):
                    wait(act, "hg_o", pr)
                    done(act.activation(OO[:, pr], PB[6 - 4 * pr][:], ACT.Copy), "hg_e", ("oo", pr))
                    done(act.activation(OS[:, pr], PB[6 - 4 * pr][:], ACT.Square), "sq2", ("hg", pr))
                for pr in range(2):
                    done(act.activation(ACC[:, 4 + pr], HG[:, pr], ACT.Tanh, scale=0.5), "hg_e", ("g", pr))
                for pr in range(2):
                    rsqrt_act(act, f"hg{pr}", 64, EPS6)
                    wait(act, "hg_small", ("y", pr))
                    done(act.activation(YH[:, 0, pr], OO[:, pr], ACT.Copy, scale=0.5), "y_hi", ("hg", pr))
                for br in BRANCHES:
                    with act.Fori(0, 4) as i:
                        for k in range(4):
                            hi_ahead(act, st, k, i, 4)
                            if k % 2 == 0:
                                lin_ready(act, st, k, i, 4)
                                b, ub = st.bank(k - 3, i, 4)
                                act.wait_ge(evac[b], ub + 1)
                                b, ub = st.bank(k, i, 4)
                                act.activation(GT[:, k // 2], PB[b][:], ACT.Tanh, scale=0.5).then_inc(evac[b], 1)
                    st.n += 16
                    st.m += 16
                s_, u_ = st.slot(-1)
                act.wait_ge(used[s_], u_ + 1)
                act.wait_ge(sem["gate_t"], HP + 32)
                for j in range(DT):
                    done(act.activation(XH[:, j], ACC[:, j], ACT.Copy), "r_hi", ("merged", j))
                split_loop(8, 8)
                evac_of(act, st.m - 2)
                evac_of(act, st.m - 1)
                squares("mixpost", ACC, SQX)
                rsqrt_act(act, "mixpost", D, EPS6)
                for j in range(DT):
                    wait(act, "hx", ("mixpost", j))
                    done(act.activation(SQX[:, j], X[:, j], ACT.Square), "sq2", ("ffnpre", j))
                rsqrt_act(act, "ffnpre", D, EPS6)
                highs("ffnpre", ACC, XH)
                for c, n in enumerate(HID):
                    hb = sum(HID[:c])

                    def pairs(i, per=4):
                        for k in range(4):
                            o = k // 2
                            hi_ahead(act, st, k, i, 4)
                            if k % 2 == 0:
                                lin_ready(act, st, k, i, 4)
                                act.wait_ge(sem["hsp"], i * 2 + (hb + o + 1))
                                b, ub = st.bank(k, i, 4)
                                act.activation(GT2[:, o], PB[b][:], ACT.Tanh, scale=0.5).then_inc(sem["gate_s"], 1)
                            else:
                                b, ub = st.bank(k, i, 4)
                                act.wait_ge(evac[b], ub + 1)
                                act.activation(H2[:, bass.ds(i * 2 + o, 1), :], HS2[:, 2 + o:3 + o], ACT.Copy, scale=0.5).then_inc(sem["h_relu"], 1)
                    with act.Fori(0, n // 2) as i:
                        pairs(i)
                    st.n += 2 * n
                    st.m += 2 * n
                    if c == 0:
                        split_loop(16, 8)
                    else:
                        with act.Fori(0, 3) as i:
                            for k in range(4):
                                hi_ahead(act, st, k, i, 4)
                        st.n += 12
                        for k in range(4):
                            hi_ahead(act, st)
                            st.n += 1
                        st.m += 8
                evac_of(act, st.m - 2)
                evac_of(act, st.m - 1)
                squares("ffnpost", ACC, SQX)
                rsqrt_act(act, "ffnpost", D, EPS6)

            split_loop(8, 8)
            ln_act(act, "ln1_0", st)
            mlp(0)
            ln_act(act, "ln2_0", st)
            ple(0)
            skip()
            wait(act, "fox_c", "neg")
            done(act.activation(FZ[:, 1], FZ[:, 1], ACT.Exp), "chain_a", "fe")
            wait(act, "chain_a", "fe")
            done(act.activation(FZ[:, 1], FZ[:, 1], ACT.Ln, bias=ONES[0:16, 0:1]), "chain_a", "fl")

            def project(j):
                pp = j % 2
                step()
                b, ub = st.bank(0)
                for e in range(2):
                    x = act.activation(QA[0:64, pp, e], PB[b][e * 64:e * 64 + 64], ACT.Copy, scale=0.125)
                x.then_inc(evac[b], 1)
                nxt()
                step()
                b, ub = st.bank(0)
                for e in range(2):
                    x = act.activation(KA[0:64, pp, e], PB[b][e * 64:e * 64 + 64], ACT.Copy)
                x.then_inc(evac[b], 1)
                nxt()
                step()
                b, ub = st.bank(0)
                if j:
                    wait(act, "misc", ("vp", j - 1))
                act.activation(VT[:], PB[b][:], ACT.Copy).then_inc(evac[b], 1)
                nxt()
            project(0)
            for j in range(8):
                if j < 7:
                    project(j + 1)
                act_attend(act, "fox", [2 * j, 2 * j + 1], 0)
            split_loop(8, 8)
            ln_act(act, "ln1_1", st)
            mlp(1)
            ln_act(act, "ln2_1", st)
            ple(1)
            second_act()
            for g in range(2):
                for k in range(TT):
                    b, ub = st.bank(0)
                    if g == 0 or k % 2:
                        wait(act, "out_t", (k, g))
                        act.activation(OUTT[:, g, k], PB[b][:], ACT.Copy).then_inc(evac[b], 1)
                    st.m += 1

        @block.vector
        def _(dve):
            st = Stream()
            for k in range(-3, 0):
                lo_ahead(dve, st, k)

            def split_in(key, j, b):
                wait(dve, "x_hi", (key, j))
                done(dve.tensor_tensor(XL[:, j], PB[b][:], XH[:, j].bitcast(F32), ALU.subtract), "x_lo", (key, j))
                dve.tensor_copy(X[:, j], PB[b][:]).then_inc(evac[b], 1)

            for j in range(DT):
                split_in("in", j, st.bank(0)[0])
                st.m += 1

            def step():
                lo_ahead(dve, st)
                lin_ready(dve, st)

            def nxt():
                st.n += 1
                st.m += 1

            def skip():
                lo_ahead(dve, st)
                nxt()

            for c in range(5):
                step()
                b, ub = st.bank(0)
                dve.tensor_copy(ACC[:, c], PB[b][:]).then_inc(evac[b], 1)
                nxt()
            wait(dve, "misc", "vec")
            done(dve.tensor_copy(VEC[:], PB[7][:, 0:P]), "misc_free", "vec")
            wait(dve, "misc", "vec2")
            done(dve.tensor_copy(VEC2[:], PB[7][:, 0:64]), "misc_free", "vec2")
            wait(dve, "misc_free", "vec2")
            g0 = VCOL["ple_b_gate", 0]
            dve.tensor_scalar(HB[:, 0:8], VEC[:, g0:g0 + 8], 0.5, None, ALU.mult)
            g0 = VCOL["ple_b_gate", 1]
            done(dve.tensor_scalar(HB[:, 8:16], VEC[:, g0:g0 + 8], 0.5, None, ALU.mult), "chain_d", "hb")

            def latent(js, key, width, gcol):
                rsqrt_dve(dve, key, width, 1e-5)
                wait(dve, "rsq", key)
                for j in js:
                    done(dve.scalar_tensor_tensor(ACC[:, j], ACC[:, j], VEC[:, gcol + j:gcol + j + 1], RS[:], ALU.mult, ALU.mult), "norm", ("c", j))
                for j in js:
                    wait(dve, "n_hi", j)
                    hi, lo = (CQH[:, j], CQL[:, j]) if j < 3 else (CKH[:, j - 3], CKL[:, j - 3])
                    done(dve.tensor_tensor(lo, ACC[:, j], hi.bitcast(F32), ALU.subtract), "n_lo", j)
            latent(range(3), "cq", 384, VCOL["ev_q_norm", 0])
            latent(range(3, 5), "ckv", 256, VCOL["ev_kv_norm", 0] - 3)
            step()
            b, ub = st.bank(0)
            dve.tensor_copy(KR[64:96, :], PB[b][0:32]).then_inc(evac[b], 1)
            m_kr = st.m
            nxt()
            COS = CST[64:96, C_COS - C_ANTI:C_COS - C_ANTI + T]
            SIN = CST[64:96, C_SIN - C_ANTI:C_SIN - C_ANTI + T]

            last_turn = []

            def rotate(dst, swap_key, out_name, out_key):
                wait(dve, "misc", swap_key)
                if last_turn:
                    wait(dve, *last_turn[-1])
                last_turn.append((out_name, out_key))
                done(dve.tensor_tensor(TMP[64:96, :], PB[7][64:96, :], SIN, ALU.mult), "misc_free", swap_key)
                done(dve.tensor_tensor(dst, dst, COS, ALU.mult), "chain_d", ("rc", swap_key))
                wait(dve, "misc_free", swap_key)
                wait(dve, "chain_d", ("rc", swap_key))
                done(dve.tensor_tensor(dst, dst, TMP[64:96, :], ALU.add), out_name, out_key)

            skip()
            evac_of(dve, m_kr)
            rotate(KR[64:96, :], "kswap", "kr", "rot")
            for c in range(3):
                skip()
            step()
            b, ub = st.bank(0)
            for e in range(2):
                for r in range(2):
                    x = dve.tensor_copy(K2[r * 64:r * 64 + 64, e], PB[b][e * 64:e * 64 + 64])
            x.then_inc(evac[b], 1)
            nxt()
            skip()

            def token_major(key, dst):
                wait(dve, "misc", key)
                done(dve.tensor_copy(dst, PB[7][:].rearrange("p (j n) -> p j n", n=P)), "misc_free", key)
            token_major("vs", VS[:])
            wait(dve, "misc", "bandv")
            done(dve.tensor_copy(BV, PB[7][0:8, 0:384]), "misc_free", "bandv")
            for h in range(8):
                step()
                b, ub = st.bank(0)
                dve.tensor_copy(Q96[:, h], PB[b][0:96]).then_inc(evac[b], 1)
                nxt()
                if h:
                    rotate(Q96[64:96, h - 1], ("qswap", h - 1), "qrope", ("rot", h - 1))
            rotate(Q96[64:96, 7], ("qswap", 7), "qrope", ("rot", 7))
            for k in range(4):
                wait(dve, "misc", ("bandt", k))
                done(dve.tensor_copy(BIAS[:, 2 * k:2 * k + 2, :], PB[7][:].rearrange("p (j n) -> p j n", n=256)), "misc_free", ("bandt", k))
            for h in range(8):
                skip()
                if h % 2:
                    token_major(("v4", h // 2), V4[:, :, h // 2 * P:h // 2 * P + P])
            dve_attend(dve, "mla", range(8), 0)
            dve_attend(dve, "swa", range(8), 4)

            def residual_loop(per_out, first=True):
                po = 4 // per_out
                with dve.Fori(0, 8 // po) as i:
                    for k in range(4):
                        lo_ahead(dve, st, k, i, 4)
                        if k % per_out == per_out - 1:
                            o = k // per_out
                            lin_ready(dve, st, k, i, 4)
                            b, ub = st.bank(o, i, po)
                            tile = bass.ds(i * po + o, 1)
                            bank = PB[b][:].unsqueeze(1)
                            if first:
                                x = dve.scalar_tensor_tensor(ACC[:, tile, :], X[:, tile, :], ALPHA, bank, ALU.mult, ALU.add)
                            else:
                                x = dve.tensor_tensor(ACC[:, tile, :], ACC[:, tile, :], bank, ALU.add)
                            x.then_inc(evac[b], 1)
                st.n += 8 * per_out
                st.m += 8

            def mlp(l):
                for half in range(2):
                    for j in range(2 * half):
                        b, ub = st.bank(0)
                        wait(dve, "pt_hi", (l, j))
                        dve.tensor_tensor(PTL[:, j], PB[b][:], PTH[:, j].bitcast(F32), ALU.subtract).then_inc(evac[b], 1)
                        st.m += 1
                    hb = (2 * l + half) * 16
                    with dve.Fori(0, 4) as i:
                        for k in range(4):
                            lo_ahead(dve, st, k, i, 4)
                            lin_ready(dve, st, k, i, 4)
                            b, ub = st.bank(k, i, 4)
                            dve.tensor_scalar(HR[:, k % 2], PB[b][:], 0.0, None, ALU.max).then_inc(evac[b], 1)
                            dve.wait_ge(sem["h_hi"], i * 4 + (hb + k + 1))
                            dve.tensor_tensor(HL[:, bass.ds(i * 4 + k, 1), :], HS[:, k % 2:k % 2 + 1], HH[:, bass.ds(i * 4 + k, 1), :].bitcast(F32), ALU.subtract).then_inc(sem["h_lo"], 1)
                    st.n += 16
                    st.m += 16
                    residual_loop(2, half == 0)

            def ple(l):
                for o in range(8):
                    lo_ahead(dve, st)
                    m_gate = st.m
                    nxt()
                    step()
                    evac_of(dve, m_gate)
                    b, ub = st.bank(0)
                    if o:
                        wait(dve, "x_new", (l, o - 1))
                    dve.scalar_tensor_tensor(GP[:, 0], GT[:, o % 2], 1.0, PB[b][:], ALU.add, ALU.mult).then_inc(evac[b], 1)
                    dve.wait_ge(evac[b], ub + 1)
                    done(dve.scalar_tensor_tensor(X[:, o], GP[:, 0], 0.5, X[:, o], ALU.mult, ALU.add), "x_new", (l, o))
                    nxt()
                if l < LAYERS - 1:
                    for j in range(DT):
                        wait(dve, "x_hi", (f"ple{l}", j))
                        done(dve.tensor_tensor(XL[:, j], X[:, j], XH[:, j].bitcast(F32), ALU.subtract), "x_lo", (f"ple{l}", j))

            def to_acc_loop(per_out, add):
                po = 4 // per_out

                def body(i, per):
                    for k in range(4):
                        lo_ahead(dve, st, k, i, per)
                        if k % per_out == per_out - 1:
                            o = k // per_out
                            lin_ready(dve, st, k, i, 4)
                            b, ub = st.bank(o, i, po)
                            tile, bank = bass.ds(i * po + o, 1), PB[b][:].unsqueeze(1)
                            if add:
                                x = dve.tensor_tensor(ACC[:, tile, :], ACC[:, tile, :], bank, ALU.add)
                            else:
                                x = dve.tensor_copy(ACC[:, tile, :], bank)
                            x.then_inc(evac[b], 1)
                n = 8 // po
                with dve.Fori(0, n - 1) as i:
                    body(i, 4)
                i = n - 1
                for k in range(4):
                    s, u = st.slot(k + 3, i, 4)
                    if 4 * u + s < total_tiles:
                        dve.wait_ge(hi_done[s], u + 1)
                        dve.tensor_tensor(WL[:, s], RAW[:, s], WH[:, s].bitcast(F32), ALU.subtract).then_inc(lo_done[s], 1)
                    if k % per_out == per_out - 1:
                        o = k // per_out
                        lin_ready(dve, st, k, i, 4)
                        b, ub = st.bank(o, i, po)
                        j = i * po + o
                        if add:
                            x = dve.tensor_tensor(ACC[:, j], ACC[:, j], PB[b][:], ALU.add)
                        else:
                            x = dve.tensor_copy(ACC[:, j], PB[b][:])
                        x.then_inc(evac[b], 1)
                st.n += 8 * per_out
                st.m += 8

            def scaled(key, src, dst, gain):
                for j in range(DT):
                    done(dve.scalar_tensor_tensor(dst[:, j], src[:, j], VEC2[:, gain + j:gain + j + 1], RS[:, 0:src.shape[-1]], ALU.mult, ALU.mult), "rn", (key, j))

            def lows(key, src, hi, lo):
                for j in range(DT):
                    wait(dve, "r_hi", (key, j))
                    done(dve.tensor_tensor(lo[:, j], src[:, j], hi[:, j].bitcast(F32), ALU.subtract), "r_lo", (key, j))

            def scaled_on(key, gain):
                for j in range(DT + 1):
                    if j < DT:
                        done(dve.scalar_tensor_tensor(ACC[:, j], ACC[:, j], VEC2[:, gain + j:gain + j + 1], RS[:], ALU.mult, ALU.mult), "rn", (key, j))
                    if j:
                        wait(dve, "rn", (key, j - 1))
                        done(dve.tensor_tensor(X[:, j - 1], X[:, j - 1], ACC[:, j - 1], ALU.add), "hx", (key, j - 1))

            chains = [0]

            def link(ins):
                chains[0] += 1
                done(ins, "chain_d", ("link", chains[0]))
                wait(dve, "chain_d", ("link", chains[0]))

            def second_dve():
                for j in range(DT):
                    wait(dve, "xt", ("mem", j))
                    b, ub = st.bank(0)
                    dve.tensor_copy(MT[:, j], PB[b][:, 0:NMEM]).then_inc(evac[b], 1)
                    st.m += 1
                rsqrt_dve(dve, "mem", D, 1e-6, NMEM)
                scaled("mem", MT, MT, V2["norm_mem_2"])
                lows("mem", MT, MH, ML)
                for c in range(4):
                    skip()
                    if c >= 2:
                        wait(dve, "misc", ("mv", c - 2))
                        done(dve.tensor_copy(MV[:, :, (c - 2) * P:(c - 1) * P], PB[7][:, 0:NMEM].rearrange("p (j n) -> p j n", n=P)), "misc_free", ("mv", c - 2))
                rsqrt_dve(dve, "mixpre", D, 1e-6)
                scaled("mixpre", X, ACC, V2["norm_mix_pre_2"])
                lows("mixpre", ACC, XH, XL)
                for c in range(4):
                    skip()
                evac_of(dve, M_MQ + 3)
                evac_of(dve, M_MQ + 2)
                wait(dve, "zeroed", "pz")
                dve.wait_ge(sem["pw_in"], 48)
                link(dve.tensor_tensor(PA[:, :, 1:528], PZ[:, :, 1:528], PZ[:, :, 0:527], ALU.add))
                link(dve.tensor_tensor(PBf[:, :, 3:528], PA[:, :, 3:528], PA[:, :, 1:526], ALU.add))
                lo, up = slice(0, 64), slice(64, 128)
                dve.tensor_tensor(PO[lo, 0], PA[lo, 0, 16:528], CNT[lo, 0], ALU.mult)
                dve.tensor_tensor(PO[up, 0], PBf[up, 0, 16:528], CNT[up, 0], ALU.mult)
                link(dve.tensor_tensor(PA[:, 1, 7:528], PBf[:, 1, 7:528], PBf[:, 1, 3:524], ALU.add))
                link(dve.tensor_tensor(PBf[:, 1, 15:528], PA[:, 1, 15:528], PA[:, 1, 7:520], ALU.add))
                dve.tensor_tensor(PO[lo, 1], PA[lo, 1, 16:528], CNT[lo, 1], ALU.mult)
                link(dve.tensor_tensor(PO[up, 1], PBf[up, 1, 16:528], CNT[up, 1], ALU.mult))
                for j in range(2):
                    done(dve.tensor_tensor(PO[:, j], PO[:, j], PZ[:, j, 16:528], ALU.subtract), "pooled", j)
                for c in range(4):
                    skip()
                for j in range(2):
                    wait(dve, "y_hi", ("pool", j))
                    g = V2["pool_scale_2"] + j
                    done(dve.scalar_tensor_tensor(YL[:, 1, j], PB[7][:], VEC2[:, g:g + 1], YH[:, 1, j].bitcast(F32), ALU.mult, ALU.subtract), "misc_free", ("pw", j))
                blocks = PB[7][:].rearrange("p (j n) -> p j n", n=P)
                skip()
                wait(dve, "misc", "iwt")
                done(dve.tensor_scalar(IWT[:], blocks[:, :, 64:72], 8 ** -0.5, None, ALU.mult), "misc_free", "iwt")
                skip()
                wait(dve, "misc", "svt")
                done(dve.tensor_copy(SV[:], blocks[:, :, 64:128]), "misc_free", "svt")
                skip()
                skip()
                dve_attend(dve, "mem", range(4), 0)
                dve.wait_ge(sem["mem_in"], 48)
                wait(dve, "misc_free", "iwt")
                for r in range(24):
                    qb, ih = r // 8 + 1, r % 8
                    w = (qb + 1) * P
                    sc, wt = SC[:, qb - 1, 0:w], IWT[:, qb, ih:ih + 1]
                    wait(dve, "ixr", r)
                    if ih == 0:
                        done(dve.tensor_scalar(sc, PR[:, r % 2, 0:w], wt, None, ALU.mult), "ixs", r)
                    else:
                        wait(dve, "ixs", r - 1)
                        done(dve.scalar_tensor_tensor(sc, PR[:, r % 2, 0:w], wt, sc, ALU.mult, ALU.add), "ixs", r)
                wait(dve, "ixs", 23)
                for qb in range(1, TT):
                    link(dve.tensor_tensor(SC[:, qb - 1, qb * P:qb * P + P], SC[:, qb - 1, qb * P:qb * P + P], CHK[:], ALU.add))

                def select_round(r):
                    for qb in range(1, TT):
                        top8 = STAT[:, 16 + 8 * qb:24 + 8 * qb]
                        done(dve.max(top8, SC[:, qb - 1, 0:(qb + 1) * P]), "topk", (r, qb, 0))
                    for qb in range(1, TT):
                        top8 = STAT[:, 16 + 8 * qb:24 + 8 * qb]
                        sc = SC[:, qb - 1, 0:(qb + 1) * P]
                        wait(dve, "topk", (r, qb, 0))
                        done(dve.match_replace(sc, top8, sc, -3e38), "topk", (r, qb, 1))
                    wait(dve, "topk", (r, TT - 1, 1))
                rnd = 0
                for c in range(12):
                    nxt()
                    if c in (8, 9):
                        wait(dve, "misc", ("hv", c - 8))
                        done(dve.tensor_copy(HV[:, :, (c - 8) * P:(c - 7) * P], blocks), "misc_free", ("hv", c - 8))
                    for _ in range(2 if c % 3 == 0 else 1):
                        select_round(rnd)
                        rnd += 1
                assert rnd * 8 == TOPN
                dve.tensor_copy(MSK[:, 0, 0:P], CHK[:])
                for qb in range(1, TT):
                    x = dve.tensor_scalar(MSK[:, qb, 0:(qb + 1) * P], SC[:, qb - 1, 0:(qb + 1) * P], -2e38, NEG, ALU.is_gt, ALU.mult)
                done(x, "topk", "mask")
                lbc = V2["lb_logits_2"]
                ends = FC[:].rearrange("p h (c n) -> p h c n", n=64)[:, :, :, 63]

                def hgrn_prepare(c):
                    if c == 0:
                        wait(dve, "hg_e", "gate")
                        link(dve.tensor_scalar(ACC[:, 0:4], ACC[:, 0:4], 1.0, None, ALU.add))
                    elif c <= 4:
                        link(dve.reciprocal(ACC[:, c - 1], ACC[:, c - 1]))
                    elif c == 5:
                        wait(dve, "hg_e", "lb")
                        link(dve.reciprocal(LBV[:, 2], LBV[:, 1]))
                        link(dve.tensor_tensor(LBV[:, 3], LBV[:, 1], LBV[:, 2], ALU.mult))
                        link(dve.tensor_tensor(LBV[:, 4], LBV[:, 3], LBV[:, 3], ALU.subtract))
                        link(dve.tensor_scalar(LBV[:, 5], LBV[:, 4], -1.0, 1.0, ALU.mult, ALU.add))
                        link(dve.tensor_scalar(LBV[:, 6], LBV[:, 5], -0.5, None, ALU.mult))
                    elif c == 6:
                        for h in range(4):
                            dve.tensor_scalar(KK[:, h], ACC[:, h], 1.0, LBV[:, 6, h:h + 1], ALU.subtract, ALU.mult)
                            x = dve.tensor_scalar(FC[:, h], ACC[:, h], LBV[:, 5, h:h + 1], LBV[:, 4, h:h + 1], ALU.mult, ALU.add)
                        link(x)
                    elif c == 7:
                        link(dve.tensor_scalar(ACC[:, 0:4], FC[:], 2.0 ** -63, None, ALU.max))
                        link(dve.tensor_scalar(FC[:], FC[:], 1e-30, 2.0 ** 63, ALU.max, ALU.mult))
                    elif c == 8:
                        done(dve.tensor_scalar(FC[:], FC[:], 1.0, None, ALU.min), "hg_small", "split")
                    elif c == 10:
                        wait(dve, "hg_e", "ln2")
                        link(dve.tensor_tensor(ACC[:, 0:4], ACC[:, 0:4], FC[:], ALU.add))
                    elif c == 11:
                        wait(dve, "zeroed", "restart")
                        for h in range(4):
                            x = dve.tensor_tensor_scan(FC[:, h], TMP[:], ACC[:, h], 0.0, ALU.mult, ALU.add)
                        done(x, "hg_small", "scan")
                        wait(dve, "hg_small", "scan")
                    elif c in (12, 13):
                        if c == 12:
                            link(dve.memset(OFF[:], 0.0))
                            link(dve.tensor_copy(OFF[:, 0], ends))
                        lv = c - 11
                        n = 1 << lv
                        for blk in range(0, 8, 2 * n):
                            for k in range(blk + n - 1, blk - 1, -1):
                                if k == blk + n - 1:
                                    link(dve.tensor_copy(OFF[:, lv, :, k], OFF[:, 0, :, k]))
                                else:
                                    link(dve.tensor_tensor(OFF[:, lv, :, k], OFF[:, 0, :, k], OFF[:, lv, :, k + 1], ALU.add))
                            for k in range(blk + n + 1, blk + 2 * n):
                                link(dve.tensor_tensor(OFF[:, lv, :, k], OFF[:, 0, :, k - 1], OFF[:, lv, :, k - 1], ALU.add))
                dve_attend(dve, "dsa", range(4), 0, hgrn_prepare)
                wait(dve, "hg_e", "tanh")
                done(dve.scalar_tensor_tensor(QQ[:], ACC[:, 0:4], 1.0, ACC[:, 4:8], ALU.add, ALU.mult), "hg_small", "qk")

                def halves(t_, lv):
                    v = t_[:].rearrange("p h (b two n) -> p (h b) two n", two=2, n=1 << lv)
                    return v[:, :, 0], v[:, :, 1]

                def decay(lv):
                    if lv:
                        wait(dve, "hg_x", (lv - 1, 1))
                    wait(dve, "hg_small", "qk")
                    if lv < 6:
                        (fl, fr), (el, er) = halves(FC, lv), halves(EE, lv)
                        n = 1 << lv
                        ref = fl[:, :, n - 1:n].to_broadcast(list(fl.shape))
                        done(dve.tensor_tensor(el, ref, fl, ALU.subtract), "hg_d", (lv, 0))
                        done(dve.tensor_tensor(er, fr, ref, ALU.subtract), "hg_d", (lv, 1))
                    else:
                        n = 1 << (lv - 6)
                        f = FC[:].rearrange("p h (b c n) -> p (h b) c n", c=2 * n, n=64)
                        e = EE[:].rearrange("p h (b c n) -> p (h b) c n", c=2 * n, n=64)
                        o = OFF[:, lv - 6].rearrange("p h (b c) -> p (h b) c", c=2 * n)
                        for c in range(2 * n):
                            oc = o[:, :, c:c + 1].to_broadcast(list(f[:, :, c].shape))
                            if c < n:
                                done(dve.tensor_tensor(e[:, :, c], oc, f[:, :, c], ALU.subtract), "hg_d", (lv, "l", c))
                            elif lv == 6:
                                done(dve.tensor_copy(e[:, :, c], f[:, :, c]), "hg_d", (lv, 1))
                            else:
                                done(dve.tensor_tensor(e[:, :, c], oc, f[:, :, c], ALU.add), "hg_d", (lv, 1) if c == 2 * n - 1 else (lv, "r", c))

                def scale_by(lv):
                    wait(dve, "hg_e", lv)
                    if lv:
                        wait(dve, "hg_prod", {7: 27, 8: 33}.get(lv, 4 * lv - 1))
                    (el, er), (xl, xr) = halves(EE, lv), halves(XX, lv)
                    done(dve.tensor_tensor(xl, el, halves(KK, lv)[0], ALU.mult), "hg_x", (lv, 0))
                    done(dve.tensor_tensor(xr, er, halves(QQ, lv)[1], ALU.mult), "hg_x", (lv, 1))

                def keep(q):
                    wait(dve, "hg_prod", q)
                    bank = PB[2 + q % 4][:].rearrange("p (h n) -> p h n", n=P)
                    if q < 32:
                        lv, a = q // 4, q % 4
                        m = LMASK[:, lv:lv + 1].bitcast(I32).to_broadcast([P, 4, P])
                        x = dve.copy_predicated(ATT[:, :, SLOT[a]], m, bank)
                    elif q < 34:
                        x = dve.tensor_copy(ATT[:, :, SLOT[2 * (q - 32)] + 1], bank)
                    else:
                        h = q - 34
                        dve.tensor_copy(ATT[:, h, 2:4], bank[:, 0:2])
                        x = dve.tensor_copy(ATT[:, h, 5:7], bank[:, 2:4])
                    done(x, "hg_read", q)
                    wait(dve, "hg_read", q)
                wait(dve, "zeroed", "att")
                dve.wait_ge(sem["tabb_in"], 32)
                decay(0)
                for lv in range(9):
                    scale_by(lv)
                    if lv < 8:
                        decay(lv + 1)
                    for q in {7: range(28, 34), 8: range(34, 38)}.get(lv, range(4 * lv, 4 * lv + 4)):
                        keep(q)
                for pr in range(2):
                    rsqrt_dve(dve, f"hg{pr}", 64, 1e-6)
                    wait(dve, "hg_e", ("g", pr))
                    g = V2["hgrn_norm_2"] + pr
                    link(dve.tensor_tensor(OO[:, pr], OO[:, pr], RS[:], ALU.mult))
                    link(dve.scalar_tensor_tensor(ACC[:, 4 + pr], ACC[:, 4 + pr], 1.0, HG[:, pr], ALU.add, ALU.mult))
                    done(dve.scalar_tensor_tensor(OO[:, pr], OO[:, pr], VEC2[:, g:g + 1], ACC[:, 4 + pr], ALU.mult, ALU.mult), "hg_small", ("y", pr))
                    wait(dve, "y_hi", ("hg", pr))
                    done(dve.scalar_tensor_tensor(YL[:, 0, pr], OO[:, pr], 0.5, YH[:, 0, pr].bitcast(F32), ALU.mult, ALU.subtract), "y_lo", ("hg", pr))
                for n, br in enumerate(BRANCHES):
                    with dve.Fori(0, 4) as i:
                        for k in range(4):
                            lo_ahead(dve, st, k, i, 4)
                            if k % 2:
                                o = k // 2
                                lin_ready(dve, st, k, i, 4)
                                b, ub = st.bank(k - 1, i, 4)
                                dve.wait_ge(evac[b], ub + 1)
                                dve.wait_ge(sem["gate_t"], i * 2 + (8 * n + o + 1))
                                b, ub = st.bank(k, i, 4)
                                dve.scalar_tensor_tensor(GP[:, o], GT[:, o], 1.0, PB[b][:], ALU.add, ALU.mult).then_inc(evac[b], 1)
                                dve.wait_ge(evac[b], ub + 1)
                                tile = ACC[:, bass.ds(i * 2 + o, 1), :]
                                gp = GP[:, o:o + 1]
                                if n:
                                    x = dve.scalar_tensor_tensor(tile, gp, 0.5, tile, ALU.mult, ALU.add)
                                else:
                                    x = dve.tensor_scalar(tile, gp, 0.5, None, ALU.mult)
                                x.then_inc(sem["gate_t"], 1)
                    st.n += 16
                    st.m += 16
                lows("merged", ACC, XH, XL)
                to_acc_loop(1, False)
                rsqrt_dve(dve, "mixpost", D, 1e-6)
                evac_of(dve, st.m - 1)
                evac_of(dve, st.m - 2)
                scaled_on("mixpost", V2["norm_mix_post_2"])
                rsqrt_dve(dve, "ffnpre", D, 1e-6)
                wait(dve, "hx", ("mixpost", DT - 1))
                scaled("ffnpre", X, ACC, V2["norm_ffn_pre_2"])
                lows("ffnpre", ACC, XH, XL)
                for c, n in enumerate(HID):
                    hb = sum(HID[:c])
                    with dve.Fori(0, n // 2) as i:
                        for k in range(4):
                            o = k // 2
                            lo_ahead(dve, st, k, i, 4)
                            b, ub = st.bank(k, i, 4)
                            if k % 2 == 0:
                                dve.wait_ge(sem["gate_s"], i * 2 + (hb + o + 1))
                                dve.wait_ge(sem["hsp"], i * 2 + (hb + o + 1))
                                dve.scalar_tensor_tensor(HS2[:, o], GT2[:, o], 1.0, PB[b][:], ALU.add, ALU.mult).then_inc(evac[b], 1)
                                dve.wait_ge(evac[b], ub + 1)
                            else:
                                lin_ready(dve, st, k, i, 4)
                                dve.tensor_tensor(HS2[:, 2 + o], HS2[:, o], PB[b][:], ALU.mult).then_inc(evac[b], 1)
                                dve.wait_ge(sem["h_relu"], i * 2 + (hb + o + 1))
                                tile = bass.ds(i * 2 + o, 1)
                                dve.scalar_tensor_tensor(L2[:, tile, :], HS2[:, 2 + o:3 + o], 0.5, H2[:, tile, :].bitcast(F32), ALU.mult, ALU.subtract).then_inc(sem["hsp"], 1)
                    st.n += 2 * n
                    st.m += 2 * n
                    to_acc_loop(2, c > 0)
                rsqrt_dve(dve, "ffnpost", D, 1e-6)
                evac_of(dve, st.m - 1)
                evac_of(dve, st.m - 2)
                scaled_on("ffnpost", V2["norm_ffn_post_2"])

            for k in range(HP):
                dve.tensor_copy(STAT[:, 44 + k:45 + k], ONES[:, 0:1]).then_inc(sem["gate_t"], 1)
                dve.tensor_copy(STAT[:, 46 + k:47 + k], ONES[:, 0:1]).then_inc(sem["hsp"], 1)
            lbc = V2["lb_logits_2"]
            done(dve.tensor_tensor(LBV[:, 0], VEC2[:, lbc:lbc + 4], VEC2[:, lbc:lbc + 4], ALU.subtract), "hg_small", "lb0")
            for k in range(HP):
                dve.tensor_copy(STAT[:, 41 + k:42 + k], ONES[:, 0:1]).then_inc(sem["h_lo"], 1)
            residual_loop(1)
            ln_dve(dve, "ln1_0", VCOL["ln1_g", 0], VCOL["ln1_b", 0])
            mlp(0)
            ln_dve(dve, "ln2_0", VCOL["ln2_g", 0], VCOL["ln2_b", 0])
            ple(0)
            step()
            b, ub = st.bank(0)
            dve.tensor_scalar(FZ[:, 0], PB[b][0:16], BF, None, ALU.add).then_inc(evac[b], 1)
            dve.wait_ge(evac[b], ub + 1)
            nxt()
            done(dve.scalar_tensor_tensor(FZ[:, 1], FZ[:, 0], -1.0, FZ[:, 0], ALU.mult, ALU.min), "fox_c", "neg")
            wait(dve, "chain_a", "fl")
            done(dve.scalar_tensor_tensor(FZ[:, 2], FZ[:, 0], 0.0, FZ[:, 1], ALU.min, ALU.subtract), "chain_d", "flog")
            wait(dve, "chain_d", "flog")
            done(dve.memset(FZ[:, 0], 1.0), "chain_d", "fone")
            wait(dve, "chain_d", "fone")
            done(dve.tensor_tensor_scan(FZ[:, 3], FZ[:, 0], FZ[:, 2], 0.0, ALU.mult, ALU.add), "fox_c", 0)
            wait(dve, "fox_c", 0)
            done(dve.tensor_scalar(FZ[:, 4], FZ[:, 3], -1.0, None, ALU.mult), "fox_c", 1)

            def project(j):
                skip()
                skip()
                skip()
                token_major(("vp", j), VP[:, j % 2])
            project(0)
            for j in range(8):
                if j < 7:
                    project(j + 1)
                dve_attend(dve, "fox", [2 * j, 2 * j + 1], 0)
            residual_loop(1)
            ln_dve(dve, "ln1_1", VCOL["ln1_g", 1], VCOL["ln1_b", 1])
            mlp(1)
            ln_dve(dve, "ln2_1", VCOL["ln2_g", 1], VCOL["ln2_b", 1])
            ple(1)
            second_dve()
            for g in range(2):
                for k in range(TT):
                    b, ub = st.bank(0)
                    if g == 1 and k % 2 == 0:
                        wait(dve, "out_t", (k, g))
                        dve.tensor_copy(OUTT[:, g, k], PB[b][:]).then_inc(evac[b], 1)
                    st.m += 1
    return cnt


_INS = ["x", "p", "rel_bias", "ev_w_in", "ev_q_norm", "ev_w_uq", "ev_kv_norm", "ev_w_ukv", "ev_sinks", "ev_w_out",
        "od_w_in", "od_b_f", "od_w_out", "ln1_g", "ln1_b", "w_up", "w_down", "ln2_g", "ln2_b", "ple_w_proj",
        "ple_w_gate", "ple_b_gate", "mem_2", "lb_logits_2", "w_in_2", "w_gate_2", "w_branch_2", "w_out_2",
        "hgrn_norm_2", "pool_w_2", "pool_scale_2", "w_mem_kv_2", "norm_mem_2", "norm_mix_pre_2", "norm_mix_post_2",
        "norm_ffn_pre_2", "norm_ffn_post_2", "w_ffn_gate_up_2", "w_ffn_down_2"]


def kernel(**inputs):
    import concourse.bacc as bacc
    from concourse.bass_utils import run_bass_kernel_spmd

    tab_a, tab_b = shape_tables()
    arrays = {n: np.ascontiguousarray(inputs[n]) for n in _INS}
    arrays["tab_a"], arrays["tab_b"] = tab_a, tab_b
    known = None
    for _ in range(2):
        nc = bacc.Bacc("TRN2", target_bir_lowering=False, num_devices=1)
        tensors = {n: nc.dram_tensor("in_" + n, a.shape, mybir.dt.from_np(a.dtype), kind="ExternalInput").ap() for n, a in arrays.items()}
        tensors["y"] = nc.dram_tensor("out_0", (1, T, D), F32, kind="ExternalOutput").ap()
        known = program(nc, known, tensors).found
    r = run_bass_kernel_spmd(nc, [{"in_" + n: a for n, a in arrays.items()}], core_ids=[0])
    return r.results[0]["out_0"]
```
